# Optimizing a Trainium2 kernel written in Bass

```python
import jax
import jax.numpy as jnp
from jax import lax
import numpy as np

D_MODEL = 1024
BATCH = 1
SEQ = 512
DEPTH = 2

GRID_W = 64
CTX_LEN = 256
N_EVEN = (DEPTH + 1) // 2
N_ODD = DEPTH // 2
EPS = 1e-6
NEG_INF = -1e30
ROPE_THETA = 10000.0
BLOCK = 128

HG_WIDTH = D_MODEL // 2
HG_HEAD_DIM = 128
HG_HEADS = HG_WIDTH // HG_HEAD_DIM
HG_CHUNK = 64

SW_HEAD_DIM = 64
SW_Q_HEADS = (D_MODEL // 2) // SW_HEAD_DIM
SW_KV_HEADS = 2
WINDOW = 128

AB_CUTS = [HG_WIDTH, 2 * HG_WIDTH, 3 * HG_WIDTH, 4 * HG_WIDTH, 5 * HG_WIDTH,
           5 * HG_WIDTH + SW_Q_HEADS * SW_HEAD_DIM,
           5 * HG_WIDTH + (SW_Q_HEADS + SW_KV_HEADS) * SW_HEAD_DIM]
AB_IN = 5 * HG_WIDTH + (SW_Q_HEADS + 2 * SW_KV_HEADS) * SW_HEAD_DIM
AB_MIX = HG_WIDTH + SW_Q_HEADS * SW_HEAD_DIM

GA_HEAD_DIM = 128
GA_Q_HEADS = D_MODEL // GA_HEAD_DIM
GA_KV_HEADS = 2
GA_CUTS = [GA_Q_HEADS * GA_HEAD_DIM, (GA_Q_HEADS + GA_KV_HEADS) * GA_HEAD_DIM]
GA_IN = (GA_Q_HEADS + 2 * GA_KV_HEADS) * GA_HEAD_DIM

PEER_HEADS = 8
PEER_N_KEYS = 128
PEER_N_EXPERTS = PEER_N_KEYS * PEER_N_KEYS
PEER_KEY_DIM = 256
PEER_HALF = PEER_KEY_DIM // 2
PEER_TOPK = 16
PEER_TOKENS = 128

kernel_name = 'hybrid_dit_hgrn2_swa_axialgqa_peer'

def _rmsnorm(x, g):
    xf = x.astype(jnp.float32)
    y = xf * lax.rsqrt(jnp.mean(xf * xf, axis=-1, keepdims=True) + EPS)
    return (y * g.astype(jnp.float32)).astype(x.dtype)

def _axial_rope_tables(n_tokens, head_dim):
    n_rows = n_tokens // GRID_W
    row = jnp.repeat(jnp.arange(n_rows), GRID_W).astype(jnp.float32)
    col = jnp.tile(jnp.arange(GRID_W), n_rows).astype(jnp.float32)
    n_freq = head_dim // 4
    inv = ROPE_THETA ** (-jnp.arange(n_freq, dtype=jnp.float32) / n_freq)
    ang = jnp.concatenate([row[:, None] * inv, col[:, None] * inv], axis=-1)
    return jnp.cos(ang), jnp.sin(ang)

def _apply_rope(x, cos, sin):
    half = x.shape[-1] // 2
    xf = x.astype(jnp.float32)
    x1, x2 = xf[..., :half], xf[..., half:]
    cs, sn = cos[:, None, :], sin[:, None, :]
    return jnp.concatenate([x1 * cs - x2 * sn, x1 * sn + x2 * cs], axis=-1).astype(x.dtype)

def _to_groups(q, k, v):
    b, l, hq, d = q.shape
    hk = k.shape[2]
    qg = q.reshape(b, l, hk, hq // hk, d).transpose(0, 2, 3, 1, 4)
    return qg, k.transpose(0, 2, 1, 3), v.transpose(0, 2, 1, 3)

def _merge_groups(o):
    b, hk, g, l, d = o.shape
    return o.transpose(0, 3, 1, 2, 4).reshape(b, l, hk * g * d)

def _softmax_attend(q, k, v, mask, sink):
    scale = q.shape[-1] ** -0.5
    s = jnp.einsum('bhgtd,bhsd->bhgts', q, k).astype(jnp.float32) * scale
    if mask is not None:
        s = jnp.where(mask, s, NEG_INF)
    if sink is None:
        p = jax.nn.softmax(s, axis=-1)
    else:
        sk = sink.astype(jnp.float32)[None, :, :, None, None]
        m = jnp.maximum(jnp.max(s, axis=-1, keepdims=True), sk)
        e = jnp.exp(s - m)
        p = e / (jnp.sum(e, axis=-1, keepdims=True) + jnp.exp(sk - m))
    return jnp.einsum('bhgts,bhsd->bhgtd', p.astype(v.dtype), v)

def _window_latent(q, k, v, kc, vc, sink):
    b, hk, g, l, d = q.shape
    nb = l // BLOCK
    pad = [(0, 0), (0, 0), (BLOCK, BLOCK), (0, 0)]
    kp, vp = jnp.pad(k, pad), jnp.pad(v, pad)
    qb = jnp.moveaxis(q.reshape(b, hk, g, nb, BLOCK, d), 3, 0)
    q_off = jnp.arange(BLOCK)
    k_off = jnp.arange(3 * BLOCK)
    ctx_mask = jnp.ones((BLOCK, kc.shape[2]), dtype=bool)

    def one(args):
        qj, j = args
        start = j * BLOCK
        kj = lax.dynamic_slice_in_dim(kp, start, 3 * BLOCK, axis=2)
        vj = lax.dynamic_slice_in_dim(vp, start, 3 * BLOCK, axis=2)
        t = start + q_off
        s = start - BLOCK + k_off
        band = (s[None, :] >= 0) & (s[None, :] < l) & (jnp.abs(t[:, None] - s[None, :]) <= WINDOW)
        mask = jnp.concatenate([ctx_mask, band], axis=1)
        return _softmax_attend(qj, jnp.concatenate([kc, kj], axis=2),
                               jnp.concatenate([vc, vj], axis=2), mask, sink)

    out = lax.map(one, (qb, jnp.arange(nb)))
    return jnp.moveaxis(out, 0, 3).reshape(b, hk, g, l, d)

def _dense_latent(q, k_all, v_all):
    b, hk, g, l, d = q.shape
    nb = l // BLOCK
    qb = jnp.moveaxis(q.reshape(b, hk, g, nb, BLOCK, d), 3, 0)
    out = lax.map(lambda qj: _softmax_attend(qj, k_all, v_all, None, None), qb)
    return jnp.moveaxis(out, 0, 3).reshape(b, hk, g, l, d)

def _hgrn_decay(f_logit, lb):
    log_f = jnp.logaddexp(jnp.log(lb), jnp.log1p(-lb) + jax.nn.log_sigmoid(f_logit.astype(jnp.float32)))
    return log_f, -jnp.expm1(log_f)

def _hg_heads(t):
    b, l, _ = t.shape
    return t.reshape(b, l, HG_HEADS, HG_HEAD_DIM).transpose(0, 2, 1, 3)

def _gla_scan(q, k, v, log_f, s0):
    b, h, t, dk = q.shape
    dv = v.shape[-1]
    n = t // HG_CHUNK
    blocks = lambda z: jnp.moveaxis(z.reshape(b, h, n, HG_CHUNK, z.shape[-1]), 2, 0)
    causal = jnp.tril(jnp.ones((HG_CHUNK, HG_CHUNK), dtype=bool))[:, :, None]

    def step(state, inp):
        qc, kc, vc, gc = inp
        cum = jnp.cumsum(gc, axis=2)
        diff = cum[:, :, :, None, :] - cum[:, :, None, :, :]
        decay = jnp.where(causal, jnp.exp(jnp.where(causal, diff, 0.0)), 0.0)
        a = jnp.einsum('bhtk,bhsk,bhtsk->bhts', qc, kc, decay)
        o = jnp.einsum('bhtk,bhkv->bhtv', qc * jnp.exp(cum), state) + jnp.einsum('bhts,bhsv->bhtv', a, vc)
        end = cum[:, :, -1:, :]
        new_state = jnp.exp(end[:, :, 0, :])[..., None] * state + \
            jnp.einsum('bhsk,bhsv->bhkv', kc * jnp.exp(end - cum), vc)
        return new_state, o

    s_fin, o = lax.scan(step, s0, (blocks(q), blocks(k), blocks(v), blocks(log_f)))
    return jnp.moveaxis(o, 0, 2).reshape(b, h, t, dv), s_fin

def _hgrn_direction(q, k, v, lf, qc, kc, vc, lfc, reverse):
    if reverse:
        q, k, v, lf, qc, kc, vc, lfc = [jnp.flip(z, axis=2) for z in (q, k, v, lf, qc, kc, vc, lfc)]
    s0 = jnp.zeros(q.shape[:2] + (HG_HEAD_DIM, HG_HEAD_DIM), jnp.float32)
    oc, s_ctx = _gla_scan(qc, kc, vc, lfc, s0)
    o, _ = _gla_scan(q, k, v, lf, s_ctx)
    if reverse:
        o, oc = jnp.flip(o, axis=2), jnp.flip(oc, axis=2)
    return o, oc

def _mixer_ab(a, ac, w_in, w_out, lb, hg_norm_g, sink, rope, need_ctx):
    b, l, _ = a.shape
    bc, lc, _ = ac.shape
    qh, ff, fb, ih, gh, qs, ks, vs = jnp.split(a @ w_in, AB_CUTS, axis=-1)
    qhc, ffc, fbc, ihc, ghc, qsc, ksc, vsc = jnp.split(ac @ w_in, AB_CUTS, axis=-1)

    def hg_prep(q_, ff_, fb_, i_):
        lf_f, k_f = _hgrn_decay(ff_, lb)
        lf_b, k_b = _hgrn_decay(fb_, lb)
        return [_hg_heads(z) for z in (jax.nn.silu(q_.astype(jnp.float32)), i_.astype(jnp.float32),
                                       lf_f, k_f, lf_b, k_b)]
    q, v, lf_f, k_f, lf_b, k_b = hg_prep(qh, ff, fb, ih)
    qc, vc, lfc_f, kc_f, lfc_b, kc_b = hg_prep(qhc, ffc, fbc, ihc)
    o_f, oc_f = _hgrn_direction(q, k_f, v, lf_f, qc, kc_f, vc, lfc_f, reverse=False)
    o_b, oc_b = _hgrn_direction(q, k_b, v, lf_b, qc, kc_b, vc, lfc_b, reverse=True)

    def hg_out(o, g, bb, ll):
        o = _rmsnorm(o, hg_norm_g).transpose(0, 2, 1, 3).reshape(bb, ll, HG_WIDTH)
        return (o * jax.nn.silu(g.astype(jnp.float32))).astype(a.dtype)

    def sw_prep(q_, k_, v_, rope_t):
        bb, ll, _ = q_.shape
        q_ = q_.reshape(bb, ll, SW_Q_HEADS, SW_HEAD_DIM)
        k_ = k_.reshape(bb, ll, SW_KV_HEADS, SW_HEAD_DIM)
        v_ = v_.reshape(bb, ll, SW_KV_HEADS, SW_HEAD_DIM)
        if rope_t is not None:
            q_, k_ = _apply_rope(q_, *rope_t), _apply_rope(k_, *rope_t)
        return _to_groups(q_, k_, v_)
    sq, sk, sv = sw_prep(qs, ks, vs, rope)
    sqc, skc, svc = sw_prep(qsc, ksc, vsc, None)
    sink_g = sink.reshape(SW_KV_HEADS, SW_Q_HEADS // SW_KV_HEADS)
    sw = _merge_groups(_window_latent(sq, sk, sv, skc, svc, sink_g)).astype(a.dtype)

    y = (jnp.concatenate([hg_out(o_f + o_b, gh, b, l), sw], axis=-1) @ w_out).astype(a.dtype)
    if not need_ctx:
        return y, None
    swc = _merge_groups(_softmax_attend(sqc, skc, svc, None, sink_g)).astype(a.dtype)
    yc = (jnp.concatenate([hg_out(oc_f + oc_b, ghc, bc, lc), swc], axis=-1) @ w_out).astype(a.dtype)
    return y, yc

def _mixer_ga(a, ac, w_in, w_out, qn_g, kn_g, rope, need_ctx):
    def prep(t, rope_t):
        bb, ll, _ = t.shape
        q_, k_, v_ = jnp.split(t @ w_in, GA_CUTS, axis=-1)
        q_ = _rmsnorm(q_.reshape(bb, ll, GA_Q_HEADS, GA_HEAD_DIM), qn_g)
        k_ = _rmsnorm(k_.reshape(bb, ll, GA_KV_HEADS, GA_HEAD_DIM), kn_g)
        v_ = v_.reshape(bb, ll, GA_KV_HEADS, GA_HEAD_DIM)
        if rope_t is not None:
            q_, k_ = _apply_rope(q_, *rope_t), _apply_rope(k_, *rope_t)
        return _to_groups(q_, k_, v_)
    q, k, v = prep(a, rope)
    qc, kc, vc = prep(ac, None)
    k_all = jnp.concatenate([kc, k], axis=2)
    v_all = jnp.concatenate([vc, v], axis=2)
    y = (_merge_groups(_dense_latent(q, k_all, v_all)) @ w_out).astype(a.dtype)
    if not need_ctx:
        return y, None
    yc = (_merge_groups(_softmax_attend(qc, kc, vc, None, None)) @ w_out).astype(a.dtype)
    return y, yc

def _peer(x, w_q, sub_keys, u, v):
    t, d = x.shape
    nb = t // PEER_TOKENS

    def one(xb):
        qh = (xb @ w_q).reshape(PEER_TOKENS, PEER_HEADS, 2, PEER_HALF)
        s = jnp.einsum('thpd,hpnd->thpn', qh, sub_keys).astype(jnp.float32)
        s1, i1 = lax.top_k(s[:, :, 0], PEER_TOPK)
        s2, i2 = lax.top_k(s[:, :, 1], PEER_TOPK)
        cand = (s1[..., :, None] + s2[..., None, :]).reshape(PEER_TOKENS, PEER_HEADS, PEER_TOPK * PEER_TOPK)
        sc, ci = lax.top_k(cand, PEER_TOPK)
        e = jnp.take_along_axis(i1, ci // PEER_TOPK, axis=-1) * PEER_N_KEYS + \
            jnp.take_along_axis(i2, ci % PEER_TOPK, axis=-1)
        gate = jax.nn.softmax(sc, axis=-1)
        ue, ve = u[e], v[e]
        act = jax.nn.gelu(jnp.einsum('thkd,td->thk', ue, xb).astype(jnp.float32), approximate=False)
        return jnp.einsum('thk,thkd->td', (gate * act).astype(ve.dtype), ve)

    return lax.map(one, x.reshape(nb, PEER_TOKENS, d)).reshape(t, d)

def _normal(k, shape, scale):
    return jax.random.normal(k, shape, jnp.float32) * scale

def setup_inputs(seed: int = 0) -> dict:
    key = jax.random.key(seed)
    ks = jax.random.split(key, 24)
    d = D_MODEL
    return {
        'x': _normal(ks[0], (BATCH, SEQ, d), 1.0),
        'c': _normal(ks[1], (BATCH, d), 1.0),
        'ctx': _normal(ks[2], (BATCH, CTX_LEN, d), 1.0),
        'c_ctx': _normal(ks[3], (d,), 1.0),
        'ada_w': _normal(ks[4], (DEPTH, d, 6 * d), 0.5 * d ** -0.5),
        'ada_b': _normal(ks[5], (DEPTH, 6 * d), 0.01),
        'norm_mix_g': 1.0 + _normal(ks[6], (DEPTH, d), 0.05),
        'norm_ffn_g': 1.0 + _normal(ks[7], (DEPTH, d), 0.05),
        'ab_w_in': _normal(ks[8], (N_EVEN, d, AB_IN), d ** -0.5),
        'ab_w_out': _normal(ks[9], (N_EVEN, AB_MIX, d), AB_MIX ** -0.5),
        'hg_lb_logits': _normal(ks[10], (N_EVEN + 1, HG_WIDTH), 1.0),
        'hg_norm_g': 1.0 + _normal(ks[11], (N_EVEN, HG_HEAD_DIM), 0.05),
        'sw_sink': _normal(ks[12], (N_EVEN, SW_Q_HEADS), 0.5),
        'ga_w_in': _normal(ks[13], (N_ODD, d, GA_IN), d ** -0.5),
        'ga_w_out': _normal(ks[14], (N_ODD, GA_Q_HEADS * GA_HEAD_DIM, d), (GA_Q_HEADS * GA_HEAD_DIM) ** -0.5),
        'ga_q_norm_g': 1.0 + _normal(ks[15], (N_ODD, GA_HEAD_DIM), 0.05),
        'ga_k_norm_g': 1.0 + _normal(ks[16], (N_ODD, GA_HEAD_DIM), 0.05),
        'peer_w_q': _normal(ks[17], (DEPTH, d, PEER_HEADS * PEER_KEY_DIM), d ** -0.5),
        'peer_sub_keys': _normal(ks[18], (DEPTH, PEER_HEADS, 2, PEER_N_KEYS, PEER_HALF), PEER_HALF ** -0.5),
        'peer_u': _normal(ks[19], (DEPTH, PEER_N_EXPERTS, d), d ** -0.5),
        'peer_v': _normal(ks[20], (DEPTH, PEER_N_EXPERTS, d), 1.0),
        'final_norm_g': 1.0 + _normal(ks[21], (d,), 0.05),
    }

def reference(x, c, ctx, c_ctx, ada_w, ada_b, norm_mix_g, norm_ffn_g,
              ab_w_in, ab_w_out, hg_lb_logits, hg_norm_g, sw_sink,
              ga_w_in, ga_w_out, ga_q_norm_g, ga_k_norm_g,
              peer_w_q, peer_sub_keys, peer_u, peer_v, final_norm_g):
    b, l, d = x.shape
    lc = ctx.shape[1]
    rope_sw = _axial_rope_tables(l, SW_HEAD_DIM)
    rope_ga = _axial_rope_tables(l, GA_HEAD_DIM)
    lbs = jnp.cumsum(jax.nn.softmax(hg_lb_logits.astype(jnp.float32), axis=0), axis=0)
    h, hc = x, ctx
    for layer in range(DEPTH):
        need_ctx = layer < DEPTH - 1
        i = layer // 2
        mod = jax.nn.silu(c) @ ada_w[layer] + ada_b[layer]
        mod_c = jax.nn.silu(c_ctx) @ ada_w[layer] + ada_b[layer]
        sh1, sc1, gt1, sh2, sc2, gt2 = jnp.split(mod[:, None, :], 6, axis=-1)
        csh1, csc1, cgt1, csh2, csc2, cgt2 = jnp.split(mod_c, 6, axis=-1)
        a = _rmsnorm(h, norm_mix_g[layer]) * (1.0 + sc1) + sh1
        ac = _rmsnorm(hc, norm_mix_g[layer]) * (1.0 + csc1) + csh1
        if layer % 2 == 0:
            y, yc = _mixer_ab(a, ac, ab_w_in[i], ab_w_out[i], lbs[i], hg_norm_g[i], sw_sink[i], rope_sw, need_ctx)
        else:
            y, yc = _mixer_ga(a, ac, ga_w_in[i], ga_w_out[i], ga_q_norm_g[i], ga_k_norm_g[i], rope_ga, need_ctx)
        h = h + gt1 * y
        f = _rmsnorm(h, norm_ffn_g[layer]) * (1.0 + sc2) + sh2
        if need_ctx:
            hc = hc + cgt1 * yc
            fc = _rmsnorm(hc, norm_ffn_g[layer]) * (1.0 + csc2) + csh2
            tokens = jnp.concatenate([f.reshape(b * l, d), fc.reshape(b * lc, d)], axis=0)
            y_all = _peer(tokens, peer_w_q[layer], peer_sub_keys[layer], peer_u[layer], peer_v[layer])
            h = h + gt2 * y_all[:b * l].reshape(b, l, d)
            hc = hc + cgt2 * y_all[b * l:].reshape(b, lc, d)
        else:
            y_f = _peer(f.reshape(b * l, d), peer_w_q[layer], peer_sub_keys[layer], peer_u[layer], peer_v[layer])
            h = h + gt2 * y_f.reshape(b, l, d)
    return _rmsnorm(h, final_norm_g)


_drawn_inputs = setup_inputs


def setup_inputs(seed=0):
    import zlib

    import numpy as np

    out = dict(_drawn_inputs(seed))
    spreads = {}
    factors = {'sw_sink': 8.0, 'ga_q_norm_g': 8.0, 'ga_k_norm_g': 8.0}
    for name, (base, spread) in spreads.items():
        noise = np.random.default_rng([zlib.crc32(name.encode()), seed]).standard_normal(out[name].shape)
        drawn = base * np.exp(spread * noise) if base else spread * noise
        out[name] = jnp.asarray(drawn.astype(out[name].dtype))
    for name, factor in factors.items():
        out[name] = (out[name] * factor).astype(out[name].dtype)
    return out
```

```python
from contextlib import ExitStack

import numpy as np

import concourse.bass as bass
from concourse import mybir

P = 128
D = 1024
DC = D // P
NX, NCTX = 512, 256
T = NX + NCTX
NT = T // P
NTX = NX // P
EPS = 1e-6

HG_HEADS = 4
HG_W = 512
FEAT0 = 21
F_Q, F_FF, F_FB, F_G, F_SQ, F_SK = 0, 4, 8, 12, 16, 20
TOK0 = HG_W + 128
FEAT1 = 10
TOK1 = 256
LEVELS = 7
SPAN = [64 >> l for l in range(LEVELS)]
FORWARD, BACKWARD = 0, 1

KEYS = 128
EXPERTS = KEYS * KEYS
PH = 8
TOPK = 16
PICKS = PH * TOPK

C_ID, C_ROT_SW, C_ROT_GA = 0, 128, 256
C_WL, C_WR, C_IOTA = 384, 512, 640
C_HGM = 672
C_SW_COS, C_SW_SIN, C_GA_COS, C_GA_SIN = 1696, 2208, 2720, 3232
C_ALL = 3744

V_C, V_BIAS, V_GMIX, V_GFFN = 0, 16, 112, 128
V_LB, V_HGN, V_GAQ, V_GAK, V_SINK = 144, 152, 153, 154, 155
V_ALL = 163

ALU = mybir.AluOpType
ACT = mybir.ActivationFunctionType
F32 = mybir.dt.float32
BF16 = mybir.dt.bfloat16
U32 = mybir.dt.uint32
AX = mybir.AxisListType.X


class Core:

    def __init__(self, nc, dram):
        self.nc = nc
        self.dram = dram
        self.phase = ""

    def opener(self, ctx, phase):
        self.phase = phase
        nc = self.nc
        taken = []

        def clear():
            nc.clear_and_free_semaphores(taken)
            nc.all_engine_barrier()

        ctx.callback(clear)

        def sb(name, shape, dt=F32):
            return ctx.enter_context(nc.sbuf_tensor(f"{phase}_{name}", shape, dt))

        def ps(name, shape, dt=F32):
            return ctx.enter_context(nc.psum_tensor(f"{phase}_{name}", shape, dt))

        def sem(name):
            taken.append(nc.alloc_semaphore(name=f"{phase}_{name}"))
            return taken[-1]

        return sb, ps, sem


def linker(engine, sem):
    count = [0]

    def link(instruction):
        count[0] += 1
        instruction.then_inc(sem, 1)
        engine.wait_ge(sem, count[0])

    return link


def wait_plain(engine, sem, value, passed):
    engine.wait_ge(sem, value)
    if not isinstance(value, int):
        engine.sem_inc(passed, 1)


def modulation(core):
    nc = core.nc
    GC = 512
    RING = 3
    GROUPS = 6 * D // GC
    MT = GC // P
    with ExitStack() as ctx:
        sb, ps, sem = core.opener(ctx, "mod")
        w = sb("w", [P, RING, DC, GC])
        silu = sb("silu", [P, DC, 2])
        tmp = sb("tmp", [P, DC, 2])
        rows = sb("rows", [96, 2, P])
        line = sb("line", [2, RING, GC])
        pm = ps("pm", [P, RING, 512])
        pc = ps("pc", [P, RING, 512])
        pt = ps("pt", [P, 2, 512])
        s_const, s_w = sem("const"), [sem(f"w{i}") for i in range(RING)]
        s_used, s_silu, s_link, s_exp = sem("used"), sem("silu"), sem("link"), sem("exp")
        s_modc, s_turned, s_rows, s_out = sem("modc"), sem("turned"), sem("rows"), sem("out")
        s_lb, s_moved, s_copied, s_cols = sem("lb"), sem("moved"), sem("copied"), sem("cols")
        s_passed = sem("passed")
        block = ctx.enter_context(nc.Block())
        ada = core.dram["ada_w"]

        @block.sync
        def _(sp):
            sp.dma_start(core.vecs[:], core.dram["vecs"]).then_inc(s_const, 16)
            sp.dma_start(core.ident[:], core.dram["consts"][:, C_ID:C_ID + P]).then_inc(s_const, 16)
            for layer in range(2):
                src = ada[layer].rearrange("(c p) n -> p c n", p=P)
                if layer == 0:
                    for s in range(RING):
                        sp.dma_start(w[:, s], src[:, :, s * GC:(s + 1) * GC]).then_inc(s_w[s], 16)
                base = layer * GROUPS
                with sp.Fori(1 if layer == 0 else 0, GROUPS // RING) as it:
                    for s in range(RING):
                        sp.wait_ge(s_used, it * RING + (base + s + 1 - RING))
                        sp.dma_start(w[:, s], src[:, :, bass.ds(it * (RING * GC) + s * GC, GC)]).then_inc(s_w[s], 16)
            for layer in range(2):
                sp.wait_ge(s_rows, layer + 1)
                sp.dma_start(core.dram["modr"][layer].rearrange("k (r q) -> (k r) q", q=P),
                             rows[:, layer, :]).then_inc(s_out, 16)
            sp.wait_ge(s_out, 32)

        @block.tensor
        def _(pe):
            pe.wait_ge(s_silu, 1)
            for layer in range(2):
                with pe.Fori(0, GROUPS // RING) as it:
                    def multiply(s):
                        pe.wait_ge(s_w[s], it * 16 + 16 * (layer * GROUPS // RING + 1))
                        pe.wait_ge(s_copied, it * RING + (layer * GROUPS + s + 1))
                        for c in range(DC):
                            last = nc.tensor.matmul(pm[0:2, s, :], silu[:, c, :], w[:, s, c, :],
                                                    start=(c == 0), stop=(c == DC - 1))
                        last.then_inc(s_used, 1)

                    def turn(s):
                        pe.wait_ge(s_copied, it * RING + (layer * GROUPS + s + 1 + RING))
                        wait_plain(pe, s_moved, it * RING + (layer * GROUPS + s + 1), s_passed)
                        for m in range(MT):
                            last = nc.tensor.transpose(pc[:, s, 2 * m:2 * m + 2], line[:, s, m * P:(m + 1) * P],
                                                       core.ident[0:2, 0:2])
                        last.then_inc(s_cols, 1)

                    multiply(0)
                    multiply(1)
                    turn(0)
                    multiply(2)
                    turn(1)
                    turn(2)
            for layer in range(2):
                pe.wait_ge(s_modc, layer + 1)
                nc.tensor.transpose(pt[0:96, layer, 0:P], core.modc[:, layer].rearrange("p k m -> p (k m)"),
                                    core.ident[:]).then_inc(s_turned, 1)

        @block.scalar
        def _(act):
            act.wait_ge(s_const, 32)
            nc.scalar.activation(tmp[:].rearrange("p c k -> p (c k)"), core.vecs[:, V_C:V_C + 16],
                                 ACT.Exp, scale=-1.0).then_inc(s_exp, 1)
            act.wait_ge(s_lb, 1)
            nc.scalar.activation(core.lbw[:, 0:8], core.lbw[:, 0:8], ACT.Exp).then_inc(s_exp, 1)

        @block.vector
        def _(dve):
            link = linker(dve, s_link)
            lbl = core.vecs[:, V_LB:V_LB + 8]
            lbw = core.lbw
            dve.wait_ge(s_const, 32)
            dve.sem_inc(s_moved, RING)
            dve.sem_inc(s_copied, RING)
            link(nc.vector.memset(core.ones[:], 1.0))
            link(nc.vector.memset(core.eps[:], EPS))
            link(nc.vector.tensor_tensor(lbw[:, 8:12], lbl[:, 0:4], lbl[:, 4:8], ALU.max))
            link(nc.vector.tensor_tensor(lbw[:, 0:4], lbl[:, 0:4], lbw[:, 8:12], ALU.subtract))
            nc.vector.tensor_tensor(lbw[:, 4:8], lbl[:, 4:8], lbw[:, 8:12], ALU.subtract).then_inc(s_lb, 1)
            t2 = tmp[:].rearrange("p c k -> p (c k)")
            dve.wait_ge(s_exp, 1)
            link(nc.vector.tensor_scalar(t2, t2, 1.0, None, ALU.add))
            link(nc.vector.reciprocal(t2, t2))
            nc.vector.tensor_tensor(silu[:].rearrange("p c k -> p (c k)"), t2, core.vecs[:, V_C:V_C + 16],
                                    ALU.mult).then_inc(s_silu, 1)
            dve.wait_ge(s_exp, 2)
            link(nc.vector.tensor_tensor(lbw[:, 8:12], lbw[:, 0:4], lbw[:, 4:8], ALU.add))
            link(nc.vector.reciprocal(lbw[:, 8:12], lbw[:, 8:12]))
            link(nc.vector.tensor_tensor(core.lb[:, 0:4], lbw[:, 0:4], lbw[:, 8:12], ALU.mult))
            link(nc.vector.tensor_scalar(core.lb[:, 4:8], core.lb[:, 0:4], -1.0, 1.0, ALU.mult, ALU.add))
            for layer in range(2):
                m = core.modc[:, layer]
                bias = V_BIAS + 48 * layer
                with dve.Fori(0, GROUPS // RING) as it:
                    def copy(s):
                        dve.wait_ge(s_used, it * RING + (layer * GROUPS + s + 1))
                        nc.vector.tensor_copy(line[:, s, :], pm[0:2, s, :]).then_inc(s_copied, 1)

                    def move(s):
                        at = it * (RING * MT) + s * MT
                        dve.wait_ge(s_cols, it * RING + (layer * GROUPS + s + 1))
                        nc.vector.tensor_tensor(m[:, :, bass.ds(at, MT)].rearrange("p k m -> p m k"),
                                                pc[:, s, 0:2 * MT].rearrange("p (m k) -> p m k", k=2),
                                                core.vecs[:, bass.ds(at + bias, MT)].unsqueeze(2).to_broadcast([P, MT, 2]),
                                                ALU.add).then_inc(s_moved, 1)

                    copy(0)
                    copy(1)
                    move(0)
                    copy(2)
                    move(1)
                    move(2)
                dve.wait_ge(s_moved, RING + (layer + 1) * GROUPS)
                for kind in range(2):
                    for part, gain in ((1, V_GMIX), (4, V_GFFN)):
                        v = m[:, kind, part * 8:part * 8 + 8]
                        last = nc.vector.scalar_tensor_tensor(
                            out=v, in0=v, scalar=1.0, in1=core.vecs[:, gain + 8 * layer:gain + 8 * layer + 8],
                            op0=ALU.add, op1=ALU.mult)
                last.then_inc(s_modc, 1)
            for layer in range(2):
                dve.wait_ge(s_turned, layer + 1)
                nc.vector.tensor_copy(rows[:, layer, :], pt[0:96, layer, 0:P]).then_inc(s_rows, 1)


def project(core, layer, feat, featT, tokV, ntok_cols, q_tiles):
    nc = core.nc
    WR = 4
    with ExitStack() as ctx:
        sb, ps, sem = core.opener(ctx, f"proj{layer}")
        h = core.h
        aT = sb("aT", [P, DC, T])
        xn = sb("xn", [P, 2, D])
        wt = sb("wt", [P, DC, ntok_cols])
        wf = sb("wf", [P, WR, DC, P])
        ssq = sb("ssq", [P, NT])
        rstd = sb("rstd", [P, NT])
        pt = ps("pt", [P, 4, 512])
        pf = ps("pf", [P, 2, 2, 512])
        s_h, s_wt, s_wf = sem("h"), sem("wt"), [sem(f"wf{i}") for i in range(WR)]
        s_ssq, s_std, s_link, s_xn = sem("ssq"), sem("std"), sem("link"), sem("xn")
        s_tr, s_aT, s_f, s_fe = sem("tr"), sem("aT"), sem("f"), [sem("fe_even"), sem("fe_odd")]
        block = ctx.enter_context(nc.Block())
        wfd, wtd = core.dram[f"wf{layer}"], core.dram[f"wt{layer}"]

        def groups(tile):
            return range(tile * 4, tile * 4 + 4)

        def evacuate(eng, i):
            kind = 0 if i < NTX else 1
            for g in groups(i):
                eng.wait_ge(s_tr, g + 1)
                for c2 in range(2):
                    c = 2 * (g % 4) + c2
                    last = nc.scalar.activation(aT[:, c, i * P:(i + 1) * P], pt[:, g % 4, c2 * P:(c2 + 1) * P],
                                                ACT.Identity, scale=core.modc[:, layer, kind, 8 + c:9 + c],
                                                bias=core.modc[:, layer, kind, c:c + 1])
                last.then_inc(s_aT, 1)

        def move_values(eng, i):
            n = feat + i
            eng.wait_ge(s_f, n + 1)
            src = pf[:, n % 2].rearrange("p a n -> p (a n)")[:, 0:ntok_cols]
            if n % 2:
                nc.vector.tensor_copy(tokV[:, i, :], src).then_inc(s_fe[1], 1)
            else:
                nc.scalar.activation(tokV[:, i, :], src, ACT.Copy).then_inc(s_fe[0], 1)

        def width(m):
            return NX if m < q_tiles else T

        def move_features(eng, m):
            eng.wait_ge(s_f, m + 1)
            src = pf[:, m % 2].rearrange("p a n -> p (a n)")[:, 0:width(m)]
            if m % 2:
                nc.vector.tensor_copy(featT[:, m, 0:width(m)], src).then_inc(s_fe[1], 1)
            else:
                nc.scalar.activation(featT[:, m, 0:width(m)], src, ACT.Copy).then_inc(s_fe[0], 1)

        @block.sync
        def _(sp):
            if layer == 0:
                sp.dma_start(h[:, 0:NTX, :], core.dram["x"].rearrange("(i p) d -> p i d", p=P)).then_inc(s_h, 16)
                sp.dma_start(h[:, NTX:NT, :], core.dram["ctx"].rearrange("(i p) d -> p i d", p=P)).then_inc(s_h, 16)
            for m in range(feat):
                if m >= WR:
                    sp.wait_ge(s_f, m - WR + 1)
                sp.dma_start(wf[:, m % WR].rearrange("p c n -> p (c n)"), wfd[m]).then_inc(s_wf[m % WR], 16)
                if m == WR - 1:
                    sp.dma_start(wt[:].rearrange("p c n -> p (c n)"), wtd).then_inc(s_wt, 16)

        @block.scalar
        def _(act):
            if layer == 0:
                act.wait_ge(s_h, 32)
            for i in range(NT):
                if i >= 2:
                    act.wait_ge(s_tr, 4 * (i - 1))
                nc.scalar.activation(xn[:, i % 2, :], h[:, i, :], ACT.Square,
                                     accum_out=ssq[:, i:i + 1]).then_inc(s_ssq, 1)
                act.wait_ge(s_ssq, i + 1)
                nc.scalar.activation(rstd[:, i:i + 1], ssq[:, i:i + 1], ACT.Sqrt, scale=1.0 / D,
                                     bias=core.eps[:]).then_inc(s_std, 1)
                if i >= 2:
                    evacuate(act, i - 2)
            evacuate(act, NT - 2)
            evacuate(act, NT - 1)
            for m in range(0, feat, 2):
                move_features(act, m)
            for i in range(NT):
                if (feat + i) % 2 == 0:
                    move_values(act, i)

        @block.vector
        def _(dve):
            link = linker(dve, s_link)
            for i in range(NT):
                dve.wait_ge(s_std, i + 1)
                link(nc.vector.reciprocal(rstd[:, i:i + 1], rstd[:, i:i + 1]))
                if i >= 2:
                    dve.wait_ge(s_tr, 4 * (i - 1))
                nc.vector.tensor_scalar(xn[:, i % 2, :], h[:, i, :], rstd[:, i:i + 1], None,
                                        ALU.mult).then_inc(s_xn, 1)
            for m in range(1, feat, 2):
                move_features(dve, m)
            for i in range(NT):
                if (feat + i) % 2:
                    move_values(dve, i)

        @block.tensor
        def _(pe):
            for i in range(NT):
                pe.wait_ge(s_xn, i + 1)
                for g in groups(i):
                    if g >= 4:
                        pe.wait_ge(s_aT, g - 3)
                    for c2 in range(2):
                        c = 2 * (g % 4) + c2
                        last = nc.tensor.transpose(pt[:, g % 4, c2 * P:(c2 + 1) * P],
                                                   xn[:, i % 2, c * P:(c + 1) * P], core.ident[:])
                    last.then_inc(s_tr, 1)
            pe.wait_ge(s_aT, 4 * NT)
            for m in range(feat):
                pe.wait_ge(s_wf[m % WR], 16 * (m // WR + 1))
                if m >= 2:
                    pe.wait_ge(s_fe[m % 2], m // 2)
                for lo, hi in ((0, NX), (NX, T)):
                    if lo >= width(m):
                        continue
                    for c in range(DC):
                        last = nc.tensor.matmul(pf[:, m % 2, lo // NX, 0:hi - lo], wf[:, m % WR, c, :],
                                                aT[:, c, lo:hi], start=(c == 0), stop=(c == DC - 1))
                last.then_inc(s_f, 1)
            pe.wait_ge(s_wt, 16)
            for i in range(NT):
                n = feat + i
                pe.wait_ge(s_fe[n % 2], n // 2)
                for lo in range(0, ntok_cols, 512):
                    hi = min(lo + 512, ntok_cols)
                    for c in range(DC):
                        last = nc.tensor.matmul(pf[:, n % 2, lo // 512, 0:hi - lo], aT[:, c, i * P:(i + 1) * P],
                                                wt[:, c, lo:hi], start=(c == 0), stop=(c == DC - 1))
                last.then_inc(s_f, 1)


def hgrn(core, featT, tokV):
    nc = core.nc
    NCH = T // P
    ORDER = {FORWARD: [4, 5, 0, 1, 2, 3], BACKWARD: [5, 4, 3, 2, 1, 0]}
    UC = 3
    UW = UC * P
    NB = 10
    BATCHES = [(0, 4), (4, 8), (8, 10)]
    with ExitStack() as ctx:
        sb, ps, sem = core.opener(ctx, "hgrn")
        hspace = core.h[:].rearrange("p i d -> p (i d)")
        state = hspace[:, 0:3072].rearrange("p (b r n v) -> p b r n v", b=2, r=2, n=6)
        qe = hspace[:, 3072:6144].rearrange("p (b r t) -> p b r t", b=2, r=2)
        kk = sb("kk", [P, 2, 2, T])
        C = sb("C", [P, 2, 2, NCH, P + 1])
        ke = sb("ke", [P, 2, T])
        kq = sb("kq", [P, 2, 2, LEVELS, UW])
        diff = sb("diff", [P, 4, UW])
        pm = sb("pm", [P, 2, 1024])
        keT = sb("keT", [P, 4, P])
        decay = sb("decay", [P, 2, 2, NCH])
        mask = sb("mask", [P, 1024])
        pP = ps("pP", [P, 2, 1024])
        pO = ps("pO", [P, 2, 512])
        pTr = ps("pTr", [P, 4, P])
        pKV = ps("pKV", [P, 4, P])
        names = ("mask", "link", "clamped", "e", "f", "g", "sum", "scaled", "kqe", "tr", "trv", "kv",
                 "state", "sub", "lexp", "kq", "P", "pm", "O", "oT", "act", "sil", "sile", "silu",
                 "sq", "ms", "std", "c0")
        S = {n: sem(n) for n in names}
        block = ctx.enter_context(nc.Block())
        flat = kq[:].rearrange("p a b l t -> p (a b l t)")
        lb, omlb = core.lb[:, 0:4], core.lb[:, 4:8]

        def silu_tiles(k):
            base = (F_Q, F_G)[k]
            return featT[:, base:base + 4, :].rearrange("p m t -> p (m t)"), flat[:, 3072 * k:3072 * k + 3072]

        def chunked(x):
            return x.rearrange("p (n t) -> p n t", t=P)

        def level_views(hb, u, r, l):
            m = SPAN[l]
            nb = P // (2 * m)
            first = 1 if r == FORWARD else 0
            c = C[:, hb, r, u * UC:(u + 1) * UC, :]
            at = c[:, :, first:first + P].rearrange("p n (b w) -> p n b w", w=2 * m)
            cut = c[:, :, m:P:2 * m].unsqueeze(3).to_broadcast([P, UC, nb, 2 * m])
            return at, cut

        def halves(x, u, m):
            v = x[:, u * UW:(u + 1) * UW].rearrange("p (b w) -> p b w", w=2 * m)
            return v[:, :, 0:m], v[:, :, m:2 * m]

        @block.sync
        def _(sp):
            sp.dma_start(mask[:], core.dram["consts"][:, C_HGM:C_HGM + 1024]).then_inc(S["mask"], 16)

        @block.gpsimd
        def _(pool):
            n = 0
            for hd in range(HG_HEADS):
                hb = hd % 2
                for u in range(2):
                    pool.wait_ge(S["sum"], hd + 1)
                    for l in range(LEVELS):
                        for r in range(2):
                            at, cut = level_views(hb, u, r, l)
                            o = diff[:, n % 4, :].rearrange("p (n b w) -> p n b w", n=UC, w=2 * SPAN[l])
                            if n >= 4:
                                pool.wait_ge(S["lexp"], n - 3)
                            nc.gpsimd.tensor_tensor(o, at, cut, ALU.subtract).then_inc(S["sub"], 1)
                            n += 1

        @block.scalar
        def _(act):
            for k in range(2):
                tile, tmp = silu_tiles(k)
                act.wait_ge(S["sil"], k + 1)
                nc.scalar.activation(tmp, tmp, ACT.Exp, scale=-1.0).then_inc(S["sile"], 1)

            def exp_logits(hd):
                act.wait_ge(S["clamped"], hd + 1)
                nc.scalar.activation(ke[:], ke[:], ACT.Exp, scale=-1.0).then_inc(S["e"], 1)

            def log_f(hd):
                act.wait_ge(S["f"], hd + 1)
                nc.scalar.activation(qe[:, hd % 2], qe[:, hd % 2], ACT.Ln).then_inc(S["g"], 1)

            def exp_sums(hd):
                hb = hd % 2
                act.wait_ge(S["sum"], hd + 1)
                last = nc.scalar.activation(ke[:, FORWARD], ke[:, FORWARD], ACT.Exp)
                last = nc.scalar.activation(qe[:, hb, BACKWARD], qe[:, hb, BACKWARD], ACT.Exp)
                last = nc.scalar.activation(chunked(ke[:, BACKWARD]), C[:, hb, BACKWARD, :, 0:P], ACT.Exp)
                last = nc.scalar.activation(chunked(qe[:, hb, FORWARD]), C[:, hb, FORWARD, :, 1:P + 1], ACT.Exp)
                last = nc.scalar.activation(decay[:, hb], C[:, hb, :, :, P], ACT.Exp)
                last.then_inc(S["scaled"], 1)

            def move_keys(hd):
                for g, (lo, hi) in enumerate(BATCHES):
                    n = hd * len(BATCHES) + g
                    act.wait_ge(S["tr"], n + 1)
                    if n > 0:
                        act.wait_ge(S["kv"], n)
                    nc.scalar.activation(keT[:, 0:hi - lo, :], pTr[:, 0:hi - lo, :], ACT.Copy).then_inc(S["trv"], 1)

            def exp_levels(hd, u):
                if hd > 0:
                    act.wait_ge(S["P"], (hd - 1) * NCH + (u + 1) * UC)
                for l in range(LEVELS):
                    m = SPAN[l]
                    keys, queries = (halves(kq[:, u, x, l, :], 0, m) for x in range(2))
                    for r in range(2):
                        n = ((hd * 2 + u) * LEVELS + l) * 2 + r
                        left, right = halves(diff[:, n % 4, :], 0, m)
                        to_left, to_right = (keys[0], queries[1]) if r == FORWARD else (queries[0], keys[1])
                        act.wait_ge(S["sub"], n + 1)
                        nc.scalar.activation(to_left, left, ACT.Exp, scale=-1.0)
                        nc.scalar.activation(to_right, right, ACT.Exp).then_inc(S["lexp"], 1)

            def move_out(n):
                hd, s = divmod(n, NCH)
                act.wait_ge(S["O"], n + 1)
                nc.scalar.activation(featT[:, F_FF + hd, s * P:(s + 1) * P], pO[:, n % 2, 0:P],
                                     ACT.Copy).then_inc(S["oT"], 1)

            exp_logits(0)
            log_f(0)
            exp_sums(0)
            move_keys(0)
            act.wait_ge(S["silu"], 2)
            for hd in range(HG_HEADS):
                more = hd + 1 < HG_HEADS
                n = hd * NCH
                exp_levels(hd, 0)
                exp_levels(hd, 1)
                if more:
                    exp_logits(hd + 1)
                move_out(n)
                move_out(n + 1)
                if more:
                    log_f(hd + 1)
                move_out(n + 2)
                if more:
                    exp_sums(hd + 1)
                move_out(n + 3)
                move_out(n + 4)
                if more:
                    move_keys(hd + 1)
                move_out(n + 5)
            for hd in range(HG_HEADS):
                act.wait_ge(S["oT"], HG_HEADS * NCH)
                nc.scalar.activation(flat[:, hd * T:(hd + 1) * T], featT[:, F_FF + hd, :],
                                     ACT.Square).then_inc(S["sq"], 1)
            for hd in range(HG_HEADS):
                act.wait_ge(S["ms"], hd + 1)
                nc.scalar.activation(flat[:, 3072 + hd * T:3072 + (hd + 1) * T], pP[:, hd % 2, 0:T], ACT.Sqrt,
                                     scale=1.0 / P, bias=core.eps[:]).then_inc(S["std"], 1)

        @block.vector
        def _(dve):
            link = linker(dve, S["link"])
            for k in range(2):
                tile, tmp = silu_tiles(k)
                nc.vector.tensor_scalar(tmp, tile, -80.0, None, ALU.max).then_inc(S["sil"], 1)
            for k in range(2):
                tile, tmp = silu_tiles(k)
                dve.wait_ge(S["sile"], k + 1)
                link(nc.vector.tensor_scalar(tmp, tmp, 1.0, None, ALU.add))
                link(nc.vector.reciprocal(tmp, tmp))
                nc.vector.tensor_tensor(tile, tile, tmp, ALU.mult).then_inc(S["silu"], 1)
            link(nc.vector.memset(C[:, :, :, :, 0], 0.0))

            def clamp_logits(hd):
                if hd > 0:
                    dve.wait_ge(S["tr"], len(BATCHES) * hd)
                for r in range(2):
                    last = nc.vector.tensor_scalar(ke[:, r], featT[:, (F_FF, F_FB)[r] + hd, :], -40.0, None, ALU.max)
                last.then_inc(S["clamped"], 1)

            def gates(hd):
                hb = hd % 2
                r_ = qe[:, hb]
                dve.wait_ge(S["e"], hd + 1)
                if hd > 1:
                    dve.wait_ge(S["O"], (hd - 1) * NCH)
                link(nc.vector.tensor_scalar(r_, ke[:], 1.0, None, ALU.add))
                link(nc.vector.reciprocal(r_, r_))
                link(nc.vector.scalar_tensor_tensor(out=kk[:, hb], in0=ke[:], scalar=omlb[:, hd:hd + 1], in1=r_,
                                                    op0=ALU.mult, op1=ALU.mult))
                nc.vector.tensor_scalar(r_, r_, omlb[:, hd:hd + 1], lb[:, hd:hd + 1], ALU.mult,
                                        ALU.add).then_inc(S["f"], 1)

            def running_sums(hd):
                hb = hd % 2
                dve.wait_ge(S["g"], hd + 1)
                for r in range(2):
                    for s in range(NCH):
                        last = nc.vector.tensor_tensor_scan(C[:, hb, r, s, 1:P + 1], core.ones[:],
                                                            qe[:, hb, r, s * P:(s + 1) * P], 0.0,
                                                            ALU.mult, ALU.add)
                link(last)
                total = C[:, hb, :, :, P:P + 1]
                nc.vector.tensor_tensor(chunked(ke[:, FORWARD]), total[:, FORWARD].to_broadcast([P, NCH, P]),
                                        C[:, hb, FORWARD, :, 1:P + 1], ALU.subtract)
                nc.vector.tensor_tensor(chunked(qe[:, hb, BACKWARD]), total[:, BACKWARD].to_broadcast([P, NCH, P]),
                                        C[:, hb, BACKWARD, :, 0:P], ALU.subtract).then_inc(S["sum"], 1)

            def scale_ends(hd):
                hb = hd % 2
                q = featT[:, F_Q + hd, :].unsqueeze(1).to_broadcast([P, 2, T])
                dve.wait_ge(S["scaled"], hd + 1)
                nc.vector.tensor_tensor(qe[:, hb], qe[:, hb], q, ALU.mult)
                nc.vector.tensor_tensor(ke[:], ke[:], kk[:, hb], ALU.mult).then_inc(S["kqe"], 1)

            def carry_states(hd):
                hb = hd % 2
                for b in range(NB):
                    r, n = divmod(b, NB // 2)
                    dve.wait_ge(S["kv"], hd * len(BATCHES) + b // 4 + 1)
                    if n == 0:
                        ins = nc.vector.tensor_copy(state[:, hb, r, 1, :], pKV[:, b % 4, :])
                    else:
                        dve.wait_ge(S["state"], hd * NB + b)
                        ins = nc.vector.scalar_tensor_tensor(
                            out=state[:, hb, r, n + 1, :], in0=state[:, hb, r, n, :],
                            scalar=decay[:, hb, r, ORDER[r][n]:ORDER[r][n] + 1],
                            in1=pKV[:, b % 4, :], op0=ALU.mult, op1=ALU.add)
                    ins.then_inc(S["state"], 1)

            def scale_levels(hd, u, levels):
                hb = hd % 2
                q = featT[:, F_Q + hd, u * UW:(u + 1) * UW]
                for l in levels:
                    m = SPAN[l]
                    left, right = halves(kq[:, u, 0, l, :], 0, m)
                    dve.wait_ge(S["lexp"], ((hd * 2 + u) * LEVELS + l) * 2 + 2)
                    nc.vector.tensor_tensor(kq[:, u, 1, l, :], kq[:, u, 1, l, :], q, ALU.mult)
                    nc.vector.tensor_tensor(left, left, halves(kk[:, hb, FORWARD], u, m)[0], ALU.mult)
                    nc.vector.tensor_tensor(right, right, halves(kk[:, hb, BACKWARD], u, m)[1],
                                            ALU.mult).then_inc(S["kq"], 1)

            def mask_pairs(n):
                dve.wait_ge(S["P"], n + 1)
                if n >= 2:
                    dve.wait_ge(S["O"], n - 1)
                nc.vector.tensor_tensor(pm[:, n % 2], pP[:, n % 2], mask[:], ALU.mult).then_inc(S["pm"], 1)

            clamp_logits(0)
            gates(0)
            running_sums(0)
            scale_ends(0)
            carry_states(0)
            dve.wait_ge(S["mask"], 16)
            for hd in range(HG_HEADS):
                more = hd + 1 < HG_HEADS
                n = hd * NCH
                scale_levels(hd, 0, range(LEVELS))
                if more:
                    clamp_logits(hd + 1)
                scale_levels(hd, 1, range(0, 4))
                mask_pairs(n)
                scale_levels(hd, 1, range(4, LEVELS))
                mask_pairs(n + 1)
                if more:
                    gates(hd + 1)
                mask_pairs(n + 2)
                if more:
                    running_sums(hd + 1)
                mask_pairs(n + 3)
                mask_pairs(n + 4)
                if more:
                    scale_ends(hd + 1)
                    carry_states(hd + 1)
                mask_pairs(n + 5)
            for hd in range(HG_HEADS):
                o = featT[:, F_FF + hd, :]
                std = flat[:, 3072 + hd * T:3072 + (hd + 1) * T]
                dve.wait_ge(S["std"], hd + 1)
                link(nc.vector.reciprocal(std, std))
                link(nc.vector.scalar_tensor_tensor(out=o, in0=o, scalar=core.vecs[:, V_HGN:V_HGN + 1], in1=std,
                                                    op0=ALU.mult, op1=ALU.mult))
                link(nc.vector.tensor_tensor(o, o, featT[:, F_G + hd, :], ALU.mult))

        @block.tensor
        def _(pe):
            def pairs(n):
                hd, s = divmod(n, NCH)
                hb, u, c = hd % 2, s // UC, s % UC
                if n >= 2:
                    pe.wait_ge(S["pm"], n - 1)
                pe.wait_ge(S["kq"], (hd * 2 + u + 1) * LEVELS)
                q = featT[:, F_Q + hd, s * P:(s + 1) * P]
                for l in range(LEVELS):
                    x = kq[:, u, :, l, c * P:(c + 1) * P]
                    nc.tensor.matmul(pP[:, n % 2, P * l:P * l + P], x[:, 0, :], x[:, 1, :], start=True, stop=True)
                for r in range(2):
                    last = nc.tensor.matmul(pP[:, n % 2, P * LEVELS:P * LEVELS + P], kk[:, hb, r, s * P:(s + 1) * P], q,
                                            start=(r == 0), stop=(r == 1))
                last.then_inc(S["P"], 1)

            def outputs(n):
                hd, s = divmod(n, NCH)
                hb = hd % 2
                o = pO[:, n % 2, 0:P]
                v = tokV[:, s, hd * P:(hd + 1) * P]
                pe.wait_ge(S["pm"], n + 1)
                pe.wait_ge(S["state"], (hd + 1) * NB)
                if n >= 2:
                    pe.wait_ge(S["oT"], n - 1)
                start = True
                for r in range(2):
                    at = ORDER[r].index(s)
                    if at > 0:
                        nc.tensor.matmul(o, state[:, hb, r, at, :], qe[:, hb, r, s * P:(s + 1) * P],
                                         start=start, stop=False)
                        start = False
                for l in range(LEVELS + 1):
                    last = nc.tensor.matmul(o, v, pm[:, n % 2, P * l:P * l + P], start=False, stop=(l == LEVELS))
                last.then_inc(S["O"], 1)

            def chunk_states(hd):
                pe.wait_ge(S["kqe"], hd + 1)
                for g, (lo, hi) in enumerate(BATCHES):
                    n = hd * len(BATCHES) + g
                    if n > 0:
                        pe.wait_ge(S["trv"], n)
                    for b in range(lo, hi):
                        r, at = divmod(b, NB // 2)
                        s = ORDER[r][at]
                        last = nc.tensor.transpose(pTr[:, b - lo, :], ke[:, r, s * P:(s + 1) * P], core.ident[:])
                    last.then_inc(S["tr"], 1)
                    pe.wait_ge(S["trv"], n + 1)
                    if n > 0:
                        pe.wait_ge(S["state"], hd * NB + lo)
                    for b in range(lo, hi):
                        r, at = divmod(b, NB // 2)
                        s = ORDER[r][at]
                        last = nc.tensor.matmul(pKV[:, b - lo, :], keT[:, b - lo, :],
                                                tokV[:, s, hd * P:(hd + 1) * P], start=True, stop=True)
                    last.then_inc(S["kv"], 1)

            chunk_states(0)
            for hd in range(HG_HEADS):
                n = hd * NCH
                pairs(n)
                for c in range(1, NCH):
                    pairs(n + c)
                    outputs(n + c - 1)
                if hd + 1 < HG_HEADS:
                    chunk_states(hd + 1)
                outputs(n + NCH - 1)
            for hd in range(HG_HEADS):
                pe.wait_ge(S["sq"], hd + 1)
                if hd >= 2:
                    pe.wait_ge(S["std"], hd - 1)
                for lo, hi in ((0, 512), (512, T)):
                    last = nc.tensor.matmul(pP[:, hd % 2, lo:hi], core.ones[:], flat[:, hd * T + lo:hd * T + hi],
                                            start=True, stop=True)
                last.then_inc(S["ms"], 1)


def attention(core, layer, featT, tokV):
    nc = core.nc
    windowed = layer == 0
    HEADS = 8
    dh = 64 if windowed else 128
    scale = float(dh) ** -0.5
    q0, k0 = (F_SQ, F_SK) if windowed else (0, 8)
    rot_tiles = list(range(q0, q0 + (5 if windowed else 10)))
    NBLK = NT if windowed else NTX
    CTX_TILES = [4, 5]

    def key_tiles(b):
        if not windowed:
            return CTX_TILES + list(range(NTX))
        if b >= NTX:
            return CTX_TILES
        return CTX_TILES + [k for k in (b - 1, b, b + 1) if 0 <= k < NTX]

    def runs(keys):
        out = []
        for n, k in enumerate(keys):
            if out and out[-1][1] + out[-1][2] == k and n % 4:
                out[-1][2] += 1
            else:
                out.append([n, k, 1])
        return out

    jobs = [(b, pos) for b in range(NBLK) for pos in range(HEADS)]
    wide = [len(key_tiles(b)) > 4 for b, _ in jobs]
    wide_before = [sum(wide[:n]) for n in range(len(jobs) + 1)]

    def head(pos):
        if windowed:
            kv = pos % 2
            return kv, q0 + pos // 2, k0, slice(HG_W + 64 * kv, HG_W + 64 * kv + 64)
        kv = pos // 4
        return kv, q0 + pos, k0 + kv, slice(P * kv, P * kv + P)

    with ExitStack() as ctx:
        sb, ps, sem = core.opener(ctx, f"att{layer}")
        rot = sb("rot", [P, P])
        cos = sb("cos", [P, NX])
        sin = sb("sin", [P, NX])
        xs = sb("xs", [P, 2, NX])
        xc = sb("xc", [P, 2, NX])
        sq = sb("sq", [P, 2, T])
        p = sb("p", [P, 2, 768])
        pT = sb("pT", [P, 2, 768])
        otok = sb("otok", [P, HEADS * dh])
        mx = sb("mx", [P, 2])
        negmax = sb("negmax", [P, 16])
        rowsum = sb("rowsum", [P, 2, HEADS])
        esink = sb("esink", [P, 2, HEADS])
        nsink = sb("nsink", [P, HEADS])
        win = sb("win", [P, 2, P], BF16)
        winf = sb("winf", [P, 2, P])
        identb = sb("identb", [P, P], BF16)
        keys2 = sb("keys2", [P, 2, T]) if windowed else None
        pS = ps("pS", [P, 2, 1024])
        pX = ps("pX", [P, 1024])
        pO = ps("pO", [P, HEADS * dh])
        names = ("const", "sq", "ms", "std", "link", "normed", "rot", "cos", "ready", "S", "nb", "exp", "T",
                 "evA", "evB", "PV", "norm", "OT", "OTe", "cast", "es")
        S = {n: sem(n) for n in names}
        block = ctx.enter_context(nc.Block())
        consts = core.dram["consts"]

        @block.sync
        def _(sp):
            rc, cc, sc = (C_ROT_SW, C_SW_COS, C_SW_SIN) if windowed else (C_ROT_GA, C_GA_COS, C_GA_SIN)
            sp.dma_start(rot[:], consts[:, rc:rc + P]).then_inc(S["const"], 16)
            sp.dma_start(cos[:], consts[:, cc:cc + NX]).then_inc(S["const"], 16)
            sp.dma_start(sin[:], consts[:, sc:sc + NX]).then_inc(S["const"], 16)
            sp.dma_start(winf[:].rearrange("p a n -> p (a n)"), consts[:, C_WL:C_WL + 2 * P]).then_inc(S["const"], 16)

        @block.gpsimd
        def _(pool):
            pool.wait_ge(S["const"], 64)
            for n, m in enumerate(rot_tiles):
                if not windowed:
                    pool.wait_ge(S["normed"], n + 1)
                if n >= 2:
                    pool.wait_ge(S["ready"], n - 1)
                nc.gpsimd.tensor_tensor(xc[:, n % 2, :], featT[:, m, 0:NX], cos[:], ALU.mult).then_inc(S["cos"], 1)

        @block.scalar
        def _(act):
            act.wait_ge(S["const"], 64)
            nc.scalar.activation(win[:].rearrange("p a n -> p (a n)"), winf[:].rearrange("p a n -> p (a n)"), ACT.Copy)
            nc.scalar.activation(identb[:], core.ident[:], ACT.Copy).then_inc(S["cast"], 1)
            if not windowed:
                for n, m in enumerate(rot_tiles):
                    w = NX if m < k0 else T
                    if n >= 2:
                        act.wait_ge(S["normed"], n - 1)
                    nc.scalar.activation(sq[:, n % 2, 0:w], featT[:, m, 0:w], ACT.Square).then_inc(S["sq"], 1)
                    act.wait_ge(S["ms"], n + 1)
                    nc.scalar.activation(sq[:, n % 2, 0:w], pS[:, n % 2, 0:w], ACT.Sqrt, scale=1.0 / dh,
                                         bias=core.eps[:]).then_inc(S["std"], 1)

            def exps(n):
                b, pos = jobs[n]
                w = len(key_tiles(b)) * P
                act.wait_ge(S["nb"], n + 1)
                if n >= 2:
                    act.wait_ge(S["T"], n - 1)
                if b >= 2:
                    act.wait_ge(S["norm"], b - 1)
                nb = negmax[:, n % 16:n % 16 + 1]
                nc.scalar.activation(p[:, n % 2, 0:w], pS[:, n % 2, 0:w], ACT.Exp, scale=scale, bias=nb,
                                     accum_out=rowsum[:, b % 2, pos:pos + 1]).then_inc(S["exp"], 1)
                if windowed:
                    nc.scalar.activation(esink[:, b % 2, pos:pos + 1], core.vecs[:, V_SINK + pos:V_SINK + pos + 1],
                                         ACT.Exp, bias=nb).then_inc(S["es"], 1)

            def move_weights(n):
                w = min(len(key_tiles(jobs[n][0])), 4) * P
                act.wait_ge(S["T"], n + 1)
                if n >= 2:
                    act.wait_ge(S["PV"], n - 1)
                nc.scalar.activation(pT[:, n % 2, 0:w], pX[:, 0:w], ACT.Copy).then_inc(S["evA"], 1)

            def move_block(b):
                act.wait_ge(S["OT"], b + 1)
                n = HEADS * dh // P
                nc.scalar.activation(featT[:, q0:q0 + n, b * P:(b + 1) * P],
                                     pX[:, 0:n * P].rearrange("p (m t) -> p m t", t=P), ACT.Copy).then_inc(S["OTe"], 1)

            exps(0)
            for n, (b, pos) in enumerate(jobs):
                if n + 1 < len(jobs):
                    exps(n + 1)
                move_weights(n)
                if pos == 0 and b > 0:
                    move_block(b - 1)
            move_block(NBLK - 1)

        @block.vector
        def _(dve):
            link = linker(dve, S["link"])
            link(nc.vector.tensor_scalar(nsink[:], core.vecs[:, V_SINK:V_SINK + HEADS], -1.0, None, ALU.mult))
            dve.wait_ge(S["const"], 64)

            def normalise(n):
                m = rot_tiles[n]
                w = NX if m < k0 else T
                x = featT[:, m, 0:w]
                gain = V_GAQ if m < k0 else V_GAK
                dve.wait_ge(S["std"], n + 1)
                link(nc.vector.reciprocal(sq[:, n % 2, 0:w], sq[:, n % 2, 0:w]))
                nc.vector.scalar_tensor_tensor(out=x, in0=x, scalar=core.vecs[:, gain:gain + 1],
                                               in1=sq[:, n % 2, 0:w], op0=ALU.mult,
                                               op1=ALU.mult).then_inc(S["normed"], 1)

            def rotate(n):
                m = rot_tiles[n]
                dve.wait_ge(S["rot"], n + 1)
                link(nc.vector.tensor_tensor(xs[:, n % 2, :], pX[:, 512 * (n % 2):512 * (n % 2) + 512], sin[:], ALU.mult))
                dve.wait_ge(S["cos"], n + 1)
                nc.vector.tensor_tensor(featT[:, m, 0:NX], xs[:, n % 2, :], xc[:, n % 2, :],
                                        ALU.add).then_inc(S["ready"], 1)

            for n in range(len(rot_tiles)):
                if not windowed:
                    normalise(n)
                if n >= 1:
                    rotate(n - 1)
            rotate(len(rot_tiles) - 1)
            if windowed:
                dve.wait_ge(S["ready"], len(rot_tiles))
                link(nc.vector.memset(keys2[:], 0.0))
                nc.vector.tensor_copy(keys2[0:64, 0, :], featT[0:64, k0, :])
                nc.vector.tensor_copy(keys2[64:128, 1, :], featT[64:128, k0, :]).then_inc(S["ready"], 1)

            def maxima(n):
                b, pos = jobs[n]
                w = len(key_tiles(b)) * P
                dve.wait_ge(S["S"], n + 1)
                link(nc.vector.tensor_reduce(mx[:, n % 2:n % 2 + 1], pS[:, n % 2, 0:w], AX, ALU.max))
                if windowed:
                    ins = nc.vector.tensor_scalar(negmax[:, n % 16:n % 16 + 1], mx[:, n % 2:n % 2 + 1], -scale,
                                                  nsink[:, pos:pos + 1], ALU.mult, ALU.min)
                else:
                    ins = nc.vector.tensor_scalar(negmax[:, n % 16:n % 16 + 1], mx[:, n % 2:n % 2 + 1], -scale,
                                                  None, ALU.mult)
                ins.then_inc(S["nb"], 1)

            def move_rest(n):
                if wide[n]:
                    w = len(key_tiles(jobs[n][0])) * P
                    dve.wait_ge(S["T"], n + 1)
                    if n >= 2:
                        dve.wait_ge(S["PV"], n - 1)
                    nc.vector.tensor_copy(pT[:, n % 2, 512:w], pX[:, 512:w]).then_inc(S["evB"], 1)

            def divide(b):
                dve.wait_ge(S["PV"], (b + 1) * HEADS)
                rs = rowsum[:, b % 2, :]
                if windowed:
                    dve.wait_ge(S["es"], (b + 1) * HEADS)
                    link(nc.vector.tensor_tensor(rs, rs, esink[:, b % 2, :], ALU.add))
                link(nc.vector.reciprocal(rs, rs))
                if b > 0:
                    dve.wait_ge(S["OT"], b)
                nc.vector.tensor_tensor(otok[:].rearrange("p (h d) -> p h d", d=dh),
                                        pO[:].rearrange("p (h d) -> p h d", d=dh),
                                        rs.unsqueeze(2).to_broadcast([P, HEADS, dh]), ALU.mult).then_inc(S["norm"], 1)

            maxima(0)
            for n, (b, pos) in enumerate(jobs):
                if n + 1 < len(jobs):
                    maxima(n + 1)
                move_rest(n)
                if pos == 0 and b > 0:
                    divide(b - 1)
            divide(NBLK - 1)

        @block.tensor
        def _(pe):
            pe.wait_ge(S["const"], 64)
            for n, m in enumerate(rot_tiles):
                if not windowed:
                    w = NX if m < k0 else T
                    pe.wait_ge(S["sq"], n + 1)
                    if n >= 2:
                        pe.wait_ge(S["std"], n - 1)
                    for lo in range(0, w, 512):
                        hi = min(lo + 512, w)
                        last = nc.tensor.matmul(pS[:, n % 2, lo:hi], core.ones[:], sq[:, n % 2, lo:hi],
                                                start=True, stop=True)
                    last.then_inc(S["ms"], 1)
                    pe.wait_ge(S["normed"], n + 1)
                if n >= 2:
                    pe.wait_ge(S["ready"], n - 1)
                nc.tensor.matmul(pX[:, 512 * (n % 2):512 * (n % 2) + 512], rot[:], featT[:, m, 0:NX],
                                 start=True, stop=True).then_inc(S["rot"], 1)
            pe.wait_ge(S["ready"], len(rot_tiles) + (1 if windowed else 0))
            pe.wait_ge(S["cast"], 1)

            def scores(n):
                b, pos = jobs[n]
                kv, qt, kt, _ = head(pos)
                keys = key_tiles(b)
                if n >= 2:
                    pe.wait_ge(S["exp"], n - 1)
                for at, k, w in runs(keys):
                    masked = [(j, 0 if keys[j] == b - 1 else 1) for j in range(at, at + w)
                              if windowed and b < NTX and k < NTX and keys[j] != b]
                    last = nc.tensor.matmul(pS[:, n % 2, at * P:(at + w) * P], featT[:, qt, b * P:(b + 1) * P],
                                            (keys2[:, kv, k * P:(k + w) * P] if windowed else
                                             featT[:, kt, k * P:(k + w) * P]), start=True, stop=not masked)
                    for x, (j, side) in enumerate(masked):
                        last = nc.tensor.matmul(pS[:, n % 2, j * P:(j + 1) * P], identb[:], win[:, side, :],
                                                start=False, stop=(x == len(masked) - 1))
                last.then_inc(S["S"], 1)

            def turn_weights(n):
                b, _ = jobs[n]
                pe.wait_ge(S["exp"], n + 1)
                if n >= 1:
                    pe.wait_ge(S["evA"], n)
                    if wide_before[n]:
                        pe.wait_ge(S["evB"], wide_before[n])
                if b > 1 or (b == 1 and jobs[n][1] > 0):
                    pe.wait_ge(S["OTe"], b if jobs[n][1] > 0 else b - 1)
                for j in range(len(key_tiles(b))):
                    last = nc.tensor.transpose(pX[:, j * P:(j + 1) * P], p[:, n % 2, j * P:(j + 1) * P], core.ident[:])
                last.then_inc(S["T"], 1)

            def values(n):
                b, pos = jobs[n]
                _, _, _, cols = head(pos)
                pe.wait_ge(S["evA"], n + 1)
                if wide[n]:
                    pe.wait_ge(S["evB"], wide_before[n + 1])
                if b > 0 and pos == 0:
                    pe.wait_ge(S["norm"], b)
                keys = key_tiles(b)
                for j, k in enumerate(keys):
                    last = nc.tensor.matmul(pO[:, pos * dh:(pos + 1) * dh], pT[:, n % 2, j * P:(j + 1) * P],
                                            tokV[:, k, cols], start=(j == 0), stop=(j == len(keys) - 1))
                last.then_inc(S["PV"], 1)

            def turn_block(b, n):
                pe.wait_ge(S["norm"], b + 1)
                pe.wait_ge(S["evA"], n)
                if wide_before[n]:
                    pe.wait_ge(S["evB"], wide_before[n])
                for j in range(HEADS * dh // P):
                    last = nc.tensor.transpose(pX[:, j * P:(j + 1) * P], otok[:, j * P:(j + 1) * P], core.ident[:])
                last.then_inc(S["OT"], 1)

            scores(0)
            scores(1)
            for n, (b, pos) in enumerate(jobs):
                turn_weights(n)
                if n + 2 < len(jobs):
                    scores(n + 2)
                values(n)
                if pos == 0 and b > 0:
                    turn_block(b - 1, n + 1)
            turn_block(NBLK - 1, len(jobs))


def out_project(core, layer, featT):
    nc = core.nc
    tiles = NT if layer == 0 else NTX
    lhs = [F_FF, F_FF + 1, F_FF + 2, F_FF + 3, F_SQ, F_SQ + 1, F_SQ + 2, F_SQ + 3] if layer == 0 else list(range(8))
    with ExitStack() as ctx:
        sb, ps, sem = core.opener(ctx, f"out{layer}")
        wo = sb("wo", [P, DC, D])
        gate = sb("gate", [P, 2, D])
        tmp = sb("tmp", [P, D])
        pY = ps("pY", [P, 2, D])
        s_w, s_g, s_h, s_y, s_t, s_ye = sem("w"), sem("g"), sem("h"), sem("y"), sem("t"), sem("ye")
        block = ctx.enter_context(nc.Block())

        @block.sync
        def _(sp):
            sp.dma_start(wo[:], core.dram[f"wo{layer}"].rearrange("(f p) n -> p f n", p=P)).then_inc(s_w, 16)
            for kind in range(2):
                row = core.dram["modr"][layer, kind, 2 * D:3 * D]
                sp.dma_start(gate[:, kind, :], row.partition_broadcast(P)).then_inc(s_g, 16)
            if layer == 0:
                sp.dma_start(core.h[:, 0:NTX, :], core.dram["x"].rearrange("(i p) d -> p i d", p=P)).then_inc(s_h, 16)
                sp.dma_start(core.h[:, NTX:NT, :], core.dram["ctx"].rearrange("(i p) d -> p i d", p=P)).then_inc(s_h, 16)

        @block.tensor
        def _(pe):
            pe.wait_ge(s_w, 16)
            for i in range(tiles):
                if i >= 2:
                    pe.wait_ge(s_ye, i - 1)
                for half in range(2):
                    for f, m in enumerate(lhs):
                        last = nc.tensor.matmul(pY[:, i % 2, half * 512:half * 512 + 512], featT[:, m, i * P:(i + 1) * P],
                                                wo[:, f, half * 512:half * 512 + 512], start=(f == 0), stop=(f == DC - 1))
                last.then_inc(s_y, 1)

        @block.vector
        def _(dve):
            dve.wait_ge(s_g, 32)
            if layer == 0:
                dve.wait_ge(s_h, 32)
            for i in range(tiles):
                dve.wait_ge(s_y, i + 1)
                if i > 0:
                    dve.wait_ge(s_t, i)
                nc.vector.tensor_tensor(tmp[:], pY[:, i % 2], gate[:, 0 if i < NTX else 1, :], ALU.mult).then_inc(s_ye, 1)
                dve.wait_ge(s_ye, i + 1)
                nc.vector.tensor_tensor(core.h[:, i, :], core.h[:, i, :], tmp[:], ALU.add).then_inc(s_t, 1)


def peer(core, layer):
    nc = core.nc
    tiles = NT if layer == 0 else NTX
    RING = 8
    GROUP = 4
    with ExitStack() as ctx:
        sb, ps, sem = core.opener(ctx, f"peer{layer}")
        h = core.h
        wq = sb("wq", [P, DC, 2 * PH * P])
        skT = sb("skT", [P, 2 * PH, KEYS])
        ring = sb("ring", [P, RING, 2 * D])
        f_cur = sb("f_cur", [P, D])
        f_next = sb("f_next", [P, D])
        rows = sb("rows", [P, 2, D])
        fT = rows[:, 0, :].rearrange("p (c t) -> p c t", t=P)
        gate_row = rows[:, 1, :]
        qT = sb("qT", [P, 2 * PH, P])
        sc = sb("sc", [P, 2 * PH, KEYS])
        diag = sb("diag", [P, 2, GROUP, P])
        top = sb("top", [P, 2 * PH, TOPK])
        topi = sb("topi", [P, 2 * PH, TOPK], U32)
        topf = sb("topf", [P, 2 * PH, TOPK])
        best = sb("best", [P, PH, TOPK])
        besti = sb("besti", [P, PICKS], U32)
        low = sb("low", [P, PICKS], U32)
        lowf = sb("lowf", [P, PICKS])
        highf = sb("highf", [P, PICKS])
        pick1 = sb("pick1", [P, PICKS])
        idx_next = sb("idx_next", [P, PICKS], U32)
        idx_cur = sb("idx_cur", [P, PICKS], U32)
        gate_next = sb("gate_next", [P, PH, TOPK])
        gate_cur = sb("gate_cur", [P, PICKS])
        gsum = sb("gsum", [P, PH])
        dots = sb("dots", [P, PICKS])
        acts = sb("acts", [P, PICKS])
        std = sb("std", [P, 2])
        iota = sb("iota", [P, 32])
        acc = ps("acc", [P, D])
        stage = ps("stage", [P, 4, 512])
        names = ("w", "iota", "rows", "gate", "ssq", "std", "fn", "tr", "fT", "q", "qT", "s", "sc", "rt", "gsub", "gexp",
                 "routed", "idxA", "idxB", "free", "dot", "gelu", "diag", "accfree", "cur", "h",
                 "passed_pool", "passed_dve")
        S = {n: sem(n) for n in names}
        landed = [sem(f"landed{i}") for i in range(RING)]
        block = ctx.enter_context(nc.Block())
        modr = core.dram["modr"]
        NEG = -3.0e38

        @block.sync
        def _(sp):
            sp.dma_start(iota[:], core.dram["consts"][:, C_IOTA:C_IOTA + 32]).then_inc(S["iota"], 16)

            def modulation_rows(tile):
                kind = 0 if tile < NTX else 1
                if tile > 0:
                    sp.wait_ge(S["q"], 4 * tile)
                    if tile > 1:
                        sp.wait_ge(S["accfree"], tile)
                for part in range(2):
                    src = modr[layer, kind, (3 + part) * D:(4 + part) * D]
                    sp.dma_start(rows[:, part, :], src.partition_broadcast(P)).then_inc(S["rows"], 16)

            def gate_rows(tile):
                kind = 0 if tile < NTX else 1
                if tile:
                    sp.wait_ge(S["accfree"], tile + 1)
                sp.wait_ge(S["fn"], min(tile + 2, tiles))
                sp.dma_start(gate_row, modr[layer, kind, 5 * D:6 * D].partition_broadcast(P)).then_inc(S["gate"], 16)

            modulation_rows(0)
            sp.dma_start(skT[:], core.dram[f"skT{layer}"].rearrange("m d n -> d m n")).then_inc(S["w"], 16)
            src = core.dram[f"wq{layer}"].rearrange("(c p) n -> p c n", p=P)
            for c in range(DC):
                sp.dma_start(wq[:, c, :], src[:, c, :]).then_inc(S["w"], 16)
            for tile in range(tiles):
                if tile + 1 < tiles:
                    modulation_rows(tile + 1)
                gate_rows(tile)

        @block.gpsimd
        def _(pool):
            def copy_half(tile, half):
                lo = 64 * half
                wait_plain(pool, S["routed"], tile + 1, S["passed_pool"])
                nc.gpsimd.tensor_copy(idx_cur[:, lo:lo + 64], idx_next[:, lo:lo + 64]).then_inc(
                    S["idxB" if half else "idxA"], 1)

            def gathers(tile, last):
                for k in range(PICKS):
                    if k == 0:
                        wait_plain(pool, S["idxA"], tile + 1, S["passed_pool"])
                    if k == 16:
                        copy_half(tile, 1)
                    if k == 64:
                        wait_plain(pool, S["idxB"], tile + 1, S["passed_pool"])
                    if k == 112 and not last:
                        copy_half(tile + 1, 0)
                    wait_plain(pool, S["free"], tile * PICKS + (k + 1), S["passed_pool"])
                    nc.gpsimd.indirect_dma_start(
                        ring[:, k % RING, :], None, core.dram[f"uv{layer}"],
                        bass.IndirectOffsetOnAxis(ap=idx_cur[:, k:k + 1], axis=0)).then_inc(landed[k % RING], 16)

            copy_half(0, 0)
            with pool.Fori(0, tiles - 1) as tile:
                gathers(tile, False)
            gathers(tiles - 1, True)

        @block.scalar
        def _(act):
            def root(tile):
                act.wait_ge(S["ssq"], tile + 1)
                nc.scalar.activation(std[:, 1:2], std[:, 0:1], ACT.Sqrt, scale=1.0 / D,
                                     bias=core.eps[:]).then_inc(S["std"], 1)

            def move_f(tile):
                act.wait_ge(S["tr"], tile + 1)
                nc.scalar.activation(rows[:, 0, :], stage[:, 0:2].rearrange("p a n -> p (a n)"),
                                     ACT.Copy).then_inc(S["fT"], 1)

            def move_q(tile, j):
                act.wait_ge(S["q"], tile * 4 + (j + 1))
                nc.scalar.activation(qT[:, 4 * j:4 * j + 4, :].rearrange("p m t -> p (m t)"), stage[:, 2 + j % 2, :],
                                     ACT.Copy).then_inc(S["qT"], 1)

            def move_scores(tile, j):
                act.wait_ge(S["s"], tile * 4 + (j + 1))
                nc.scalar.activation(sc[:, 4 * j:4 * j + 4, :].rearrange("p m t -> p (m t)"), stage[:, j % 2, :],
                                     ACT.Copy).then_inc(S["sc"], 1)

            def gate_exp(tile):
                act.wait_ge(S["gsub"], tile + 1)
                nc.scalar.activation(gate_next[:], gate_next[:], ACT.Exp).then_inc(S["gexp"], 1)

            def experts(tile, route):
                for k in range(PICKS):
                    if route:
                        if k == 10:
                            root(tile + 1)
                        if k == 22:
                            move_f(tile + 1)
                        if k in (32, 36, 40, 44):
                            move_q(tile + 1, (k - 32) // 4)
                        if k in (52, 54, 56, 58):
                            move_scores(tile + 1, (k - 52) // 2)
                        if k == 92:
                            gate_exp(tile + 1)
                    if k % GROUP == GROUP - 1:
                        g = k - GROUP + 1
                        act.wait_ge(S["dot"], tile * PICKS + (k + 1))
                        nc.scalar.activation(acts[:, g:k + 1], dots[:, g:k + 1], ACT.Gelu).then_inc(S["gelu"], 1)

            root(0)
            move_f(0)
            for j in range(4):
                move_q(0, j)
            for j in range(4):
                move_scores(0, j)
            gate_exp(0)
            with act.Fori(0, tiles - 1) as tile:
                experts(tile, True)
            experts(tiles - 1, False)

        @block.vector
        def _(dve):
            STEPS = 24

            def linker_of(tile):
                count = [0]

                def link(ins):
                    count[0] += 1
                    ins.then_inc(S["rt"], 1)
                    wait_plain(dve, S["rt"], tile * STEPS + count[0], S["passed_dve"])

                return link, count

            def dyn(x, tile):
                return x[:, tile, :] if isinstance(tile, int) else x[:, bass.ds(tile, 1), :].rearrange("p a d -> p (a d)")

            def squares(tile, link):
                if not isinstance(tile, int):
                    dve.wait_ge(S["tr"], tile)
                nc.vector.scalar_tensor_tensor(out=f_next[:], in0=dyn(h, tile), scalar=1.0, in1=dyn(h, tile),
                                               op0=ALU.mult, op1=ALU.mult, accum_out=std[:, 0:1]).then_inc(S["ssq"], 1)

            def normalise(tile, link):
                wait_plain(dve, S["std"], tile + 1, S["passed_dve"])
                link(nc.vector.reciprocal(std[:, 1:2], std[:, 1:2]))
                dve.wait_ge(S["rows"], tile * 32 + 32)
                link(nc.vector.scalar_tensor_tensor(out=f_next[:], in0=dyn(h, tile), scalar=std[:, 1:2],
                                                    in1=rows[:, 1, :], op0=ALU.mult, op1=ALU.mult))
                nc.vector.tensor_tensor(f_next[:], f_next[:], rows[:, 0, :], ALU.add).then_inc(S["fn"], 1)

            def best8(dst, src, count):
                for m in range(count):
                    last = nc.vector.max(dst(m), src(m))
                return last

            def scores_of(m):
                return sc[:, m, :]

            def search_keys(tile, link, step):
                if step == 0:
                    wait_plain(dve, S["sc"], tile * 4 + 4, S["passed_dve"])
                    link(best8(lambda m: top[:, m, 0:8], scores_of, 2 * PH))
                if step == 1:
                    for m in range(2 * PH):
                        last = nc.vector.max_index(topi[:, m, 0:8], top[:, m, 0:8], sc[:, m, :])
                    link(last)
                if step == 2:
                    for m in range(2 * PH):
                        last = nc.vector.match_replace(sc[:, m, :], top[:, m, 0:8], sc[:, m, :], NEG)
                    link(last)
                if step == 3:
                    link(best8(lambda m: top[:, m, 8:16], scores_of, 2 * PH))
                if step == 4:
                    for m in range(2 * PH):
                        last = nc.vector.max_index(topi[:, m, 8:16], top[:, m, 8:16], sc[:, m, :])
                    link(last)
                    nc.vector.tensor_copy(topf[:], topi[:])

            cand = sc[:].rearrange("p m n -> p (m n)").rearrange("p (h n) -> p h n", n=TOPK * TOPK)
            by_head = top[:].rearrange("p (h s) k -> p h s k", s=2)
            fkeys = topf[:].rearrange("p (h s) k -> p h s k", s=2)

            def search_candidates(tile, link, step):
                if step == 0:
                    link(nc.vector.tensor_tensor(
                        cand.rearrange("p h (a b) -> p h a b", b=TOPK),
                        by_head[:, :, 0, :].unsqueeze(3).to_broadcast([P, PH, TOPK, TOPK]),
                        by_head[:, :, 1, :].unsqueeze(2).to_broadcast([P, PH, TOPK, TOPK]), ALU.add))
                if step == 1:
                    link(best8(lambda m: best[:, m, 0:8], lambda m: cand[:, m, :], PH))
                if step == 2:
                    for m in range(PH):
                        last = nc.vector.max_index(besti[:, m * TOPK:m * TOPK + 8], best[:, m, 0:8], cand[:, m, :])
                    link(last)
                if step == 3:
                    for m in range(PH):
                        last = nc.vector.match_replace(cand[:, m, :], best[:, m, 0:8], cand[:, m, :], NEG)
                    link(last)
                if step == 4:
                    link(best8(lambda m: best[:, m, 8:16], lambda m: cand[:, m, :], PH))
                if step == 5:
                    for m in range(PH):
                        last = nc.vector.max_index(besti[:, m * TOPK + 8:m * TOPK + 16], best[:, m, 8:16],
                                                   cand[:, m, :])
                    link(last)

            def softmax_in(tile):
                nc.vector.tensor_tensor(gate_next[:], best[:], best[:, :, 0:1].to_broadcast([P, PH, TOPK]),
                                        ALU.subtract).then_inc(S["gsub"], 1)

            def decode(tile, link, step):
                onehot = sc[:].rearrange("p m n -> p (m n)").rearrange("p (k j) -> p k j", j=TOPK)
                byh = onehot.rearrange("p (h k) j -> p h k j", k=TOPK)
                if step == 0:
                    nc.vector.tensor_scalar(low[:], besti[:], TOPK - 1, None, ALU.bitwise_and)
                    link(nc.vector.tensor_copy(highf[:], besti[:]))
                    link(nc.vector.tensor_copy(lowf[:], low[:]))
                    link(nc.vector.tensor_tensor(highf[:], highf[:], lowf[:], ALU.subtract))
                if step in (1, 2):
                    side = step - 1
                    which = (highf, lowf)[side]
                    code = iota[:, 16 * side:16 * side + 16]
                    link(nc.vector.tensor_tensor(onehot, which[:].unsqueeze(2).to_broadcast([P, PICKS, TOPK]),
                                                 code.unsqueeze(1).to_broadcast([P, PICKS, TOPK]), ALU.is_equal))
                    link(nc.vector.tensor_tensor(byh, byh, fkeys[:, :, side, :].unsqueeze(2).to_broadcast(
                        [P, PH, TOPK, TOPK]), ALU.mult))
                    link(nc.vector.tensor_reduce((pick1, lowf)[side][:], onehot, AX, ALU.add))

            def finish_routing(tile, link, count):
                wait_plain(dve, S["gexp"], tile + 1, S["passed_dve"])
                if not isinstance(tile, int):
                    wait_plain(dve, S["idxB"], tile, S["passed_dve"])
                link(nc.vector.tensor_reduce(gsum[:], gate_next[:], AX, ALU.add))
                nc.vector.reciprocal(gsum[:], gsum[:]).then_inc(S["rt"], 1)
                count[0] += 1
                dve.wait_ge(S["rt"], tile * STEPS + count[0])
                nc.vector.tensor_tensor(gate_next[:], gate_next[:],
                                        gsum[:].unsqueeze(2).to_broadcast([P, PH, TOPK]), ALU.mult)
                nc.vector.scalar_tensor_tensor(out=idx_next[:], in0=pick1[:], scalar=float(KEYS), in1=lowf[:],
                                               op0=ALU.mult, op1=ALU.add).then_inc(S["routed"], 1)

            def take_over(tile):
                wait_plain(dve, S["routed"], tile + 1, S["passed_dve"])
                if not isinstance(tile, int):
                    dve.wait_ge(S["h"], tile)
                nc.vector.tensor_copy(f_cur[:], f_next[:])
                nc.vector.tensor_copy(gate_cur[:], gate_next[:].rearrange("p h k -> p (h k)")).then_inc(S["cur"], 1)

            def diagonals(tile, g):
                n = tile * (PICKS // GROUP) + (g + 1)
                dve.wait_ge(S["gelu"], n)
                dve.wait_ge(S["free"], tile * PICKS + (g * GROUP + RING - GROUP))
                for j in range(GROUP):
                    k = g * GROUP + j
                    last = nc.vector.tensor_scalar(diag[:, g % 2, j, :], core.ident[:], acts[:, k:k + 1],
                                                   gate_cur[:, k:k + 1], ALU.mult, ALU.mult)
                last.then_inc(S["diag"], 1)

            def end_tile(tile):
                dve.wait_ge(S["free"], tile * PICKS + (PICKS + RING))
                dve.wait_ge(S["gate"], tile * 16 + 16)
                nc.vector.tensor_tensor(f_cur[:], acc[:], gate_row, ALU.mult).then_inc(S["accfree"], 1)
                dve.wait_ge(S["accfree"], tile + 2)
                nc.vector.tensor_tensor(dyn(h, tile), dyn(h, tile), f_cur[:], ALU.add).then_inc(S["h"], 1)

            def experts(tile, route):
                if route:
                    link, count = linker_of(tile + 1)
                dve.wait_ge(S["cur"], tile + 1)
                for k in range(PICKS):
                    if route:
                        nxt = tile + 1
                        if k == 6:
                            squares(nxt, link)
                        if k == 14:
                            normalise(nxt, link)
                        if 62 <= k < 72 and k % 2 == 0:
                            search_keys(nxt, link, (k - 62) // 2)
                        if 72 <= k < 84 and k % 2 == 0:
                            search_candidates(nxt, link, (k - 72) // 2)
                        if k == 84:
                            softmax_in(nxt)
                        if k in (86, 88, 90):
                            decode(nxt, link, (k - 86) // 2)
                        if k == 96:
                            finish_routing(nxt, link, count)
                            assert count[0] == STEPS, count
                    dve.wait_ge(landed[k % RING], tile * (PICKS // RING * 16) + 16 * (k // RING + 1))
                    slot = ring[:, k % RING, 0:D]
                    nc.vector.tensor_tensor_reduce(slot, slot, f_cur[:], 1.0, 0.0, ALU.mult, ALU.add,
                                                   dots[:, k:k + 1]).then_inc(S["dot"], 1)
                    if k % GROUP == 0 and k > 0:
                        diagonals(tile, k // GROUP - 1)
                diagonals(tile, PICKS // GROUP - 1)
                end_tile(tile)
                if route:
                    take_over(tile + 1)

            dve.sem_inc(S["accfree"], 1)
            dve.sem_inc(S["free"], RING)
            dve.wait_ge(S["iota"], 16)
            link, count = linker_of(0)
            squares(0, link)
            normalise(0, link)
            for step in range(5):
                search_keys(0, link, step)
            for step in range(6):
                search_candidates(0, link, step)
            softmax_in(0)
            for step in range(3):
                decode(0, link, step)
            finish_routing(0, link, count)
            take_over(0)
            with dve.Fori(0, tiles - 1) as tile:
                experts(tile, True)
            experts(tiles - 1, False)

        @block.tensor
        def _(pe):
            def turn_f(tile):
                pe.wait_ge(S["fn"], tile + 1)
                for c in range(DC):
                    last = nc.tensor.transpose(stage[:, c // 4, (c % 4) * P:(c % 4 + 1) * P],
                                               f_next[:, c * P:(c + 1) * P], core.ident[:])
                last.then_inc(S["tr"], 1)

            def queries(tile, m):
                if m == 0:
                    pe.wait_ge(S["fT"], tile + 1)
                if m % 4 == 0 and m >= 8:
                    pe.wait_ge(S["qT"], tile * 4 + (m // 4 - 1))
                for c in range(DC):
                    last = nc.tensor.matmul(stage[:, 2 + (m // 4) % 2, (m % 4) * P:(m % 4 + 1) * P],
                                            wq[:, c, m * P:(m + 1) * P], fT[:, c, :], start=(c == 0), stop=(c == DC - 1))
                if m % 4 == 3:
                    last.then_inc(S["q"], 1)

            def key_scores(tile, j):
                pe.wait_ge(S["qT"], tile * 4 + (j + 1))
                if j >= 2:
                    pe.wait_ge(S["sc"], tile * 4 + (j - 1))
                for m in range(4 * j, 4 * j + 4):
                    last = nc.tensor.matmul(stage[:, j % 2, (m % 4) * P:(m % 4 + 1) * P], qT[:, m, :], skT[:, m, :],
                                            start=True, stop=True)
                last.then_inc(S["s"], 1)

            def experts(tile, route):
                pe.wait_ge(S["accfree"], tile + 1)
                for k in range(PICKS):
                    if route:
                        if k == 18:
                            turn_f(tile + 1)
                        if 26 <= k < 42:
                            queries(tile + 1, k - 26)
                        if k in (48, 50, 52, 54):
                            key_scores(tile + 1, (k - 48) // 2)
                    if k % GROUP == 0:
                        pe.wait_ge(S["diag"], tile * (PICKS // GROUP) + (k // GROUP + 1))
                    for half in range(2):
                        last = nc.tensor.matmul(acc[:, half * 512:half * 512 + 512], diag[:, (k // GROUP) % 2, k % GROUP, :],
                                                ring[:, k % RING, D + half * 512:D + half * 512 + 512],
                                                start=(k == 0), stop=(k == PICKS - 1))
                    last.then_inc(S["free"], 1)

            pe.wait_ge(S["w"], 16 * (1 + DC))
            turn_f(0)
            for m in range(2 * PH):
                queries(0, m)
            for j in range(4):
                key_scores(0, j)
            with pe.Fori(0, tiles - 1) as tile:
                experts(tile, True)
            experts(tiles - 1, False)


def final_norm(core):
    nc = core.nc
    with ExitStack() as ctx:
        sb, ps, sem = core.opener(ctx, "fin")
        gain = sb("gain", [P, D])
        out = sb("out", [P, NTX, D])
        ssq = sb("ssq", [P, NTX])
        s_gain, s_ssq, s_std, s_link, s_y, s_out = (sem(n) for n in ("gain", "ssq", "std", "link", "y", "out"))
        block = ctx.enter_context(nc.Block())

        @block.sync
        def _(sp):
            sp.dma_start(gain[:], core.dram["final_g"].partition_broadcast(P)).then_inc(s_gain, 16)
            dst = core.dram["out"].rearrange("(i p) d -> p i d", p=P)
            for i in range(NTX):
                sp.wait_ge(s_y, i + 1)
                sp.dma_start(dst[:, i, :], out[:, i, :]).then_inc(s_out, 16)
            sp.wait_ge(s_out, 16 * NTX)

        @block.scalar
        def _(act):
            for i in range(NTX):
                nc.scalar.activation(out[:, i, :], core.h[:, i, :], ACT.Square,
                                     accum_out=ssq[:, i:i + 1]).then_inc(s_ssq, 1)
            act.wait_ge(s_ssq, NTX)
            nc.scalar.activation(ssq[:], ssq[:], ACT.Sqrt, scale=1.0 / D, bias=core.eps[:]).then_inc(s_std, 1)

        @block.vector
        def _(dve):
            link = linker(dve, s_link)
            dve.wait_ge(s_std, 1)
            link(nc.vector.reciprocal(ssq[:], ssq[:]))
            dve.wait_ge(s_gain, 16)
            for i in range(NTX):
                nc.vector.scalar_tensor_tensor(out=out[:, i, :], in0=core.h[:, i, :], scalar=ssq[:, i:i + 1],
                                               in1=gain[:], op0=ALU.mult, op1=ALU.mult).then_inc(s_y, 1)


PHASES = ("mod", "proj0", "hgrn", "att0", "out0", "peer0", "proj1", "att1", "out1", "peer1", "fin")


def trunk(nc, dram, phases=PHASES):
    core = Core(nc, dram)
    with ExitStack() as ctx:
        def keep(name, shape):
            return ctx.enter_context(nc.sbuf_tensor(name, shape, F32))

        core.h = keep("h", [P, NT, D])
        core.vecs = keep("vecs", [P, V_ALL])
        core.ident = keep("ident", [P, P])
        core.ones = keep("ones", [P, P])
        core.eps = keep("eps", [P, 1])
        core.modc = keep("modc", [P, 2, 2, 48])
        core.lb = keep("lb", [P, 8])
        core.lbw = keep("lbw", [P, 12])
        if "mod" in phases:
            modulation(core)
        with ExitStack() as layer:
            featT = layer.enter_context(nc.sbuf_tensor("featT0", [P, FEAT0, T], F32))
            tokV = layer.enter_context(nc.sbuf_tensor("tokV0", [P, NT, TOK0], F32))
            if "proj0" in phases:
                project(core, 0, FEAT0, featT, tokV, TOK0, 0)
            if "hgrn" in phases:
                hgrn(core, featT, tokV)
            if "att0" in phases:
                attention(core, 0, featT, tokV)
            if "out0" in phases:
                out_project(core, 0, featT)
        if "peer0" in phases:
            peer(core, 0)
        with ExitStack() as layer:
            featT = layer.enter_context(nc.sbuf_tensor("featT1", [P, FEAT1, T], F32))
            tokV = layer.enter_context(nc.sbuf_tensor("tokV1", [P, NT, TOK1], F32))
            if "proj1" in phases:
                project(core, 1, FEAT1, featT, tokV, TOK1, 8)
            if "att1" in phases:
                attention(core, 1, featT, tokV)
            if "out1" in phases:
                out_project(core, 1, featT)
        if "peer1" in phases:
            peer(core, 1)
        if "fin" in phases:
            final_norm(core)


def shape_constants():
    c = np.zeros((P, C_ALL), np.float32)
    c[:, C_ID:C_ID + P] = np.eye(P)
    for base, head in ((C_ROT_SW, 64), (C_ROT_GA, 128)):
        half = head // 2
        for m in range(P):
            if m % head < half:
                c[m + half, base + m] = -1.0
            else:
                c[m - half, base + m] = 1.0
    t, s = np.arange(P)[:, None], np.arange(P)[None, :]
    c[:, C_WL:C_WL + P] = np.where(s >= t, 0.0, -1e30)
    c[:, C_WR:C_WR + P] = np.where(s <= t, 0.0, -1e30)
    c[:, C_IOTA:C_IOTA + 16] = 16.0 * np.arange(16)
    c[:, C_IOTA + 16:C_IOTA + 32] = np.arange(16)
    key = np.arange(P)
    for l, m in enumerate(SPAN):
        same, half = key // (2 * m), key // m
        c[:, C_HGM + P * l:C_HGM + P * l + P] = (same[:, None] == same) & (half[:, None] != half)
    c[:, C_HGM + P * LEVELS:C_HGM + P * LEVELS + P] = np.eye(P)
    tok = np.arange(NX)
    row, colm = (tok // 64).astype(np.float32), (tok % 64).astype(np.float32)
    for head, cc, cs in ((64, C_SW_COS, C_SW_SIN), (128, C_GA_COS, C_GA_SIN)):
        nf = head // 4
        inv = np.float32(10000.0) ** (-np.arange(nf, dtype=np.float32) / np.float32(nf))
        ang = np.concatenate([row[:, None] * inv, colm[:, None] * inv], axis=-1).T
        ang = np.tile(ang, (P // (head // 2), 1))
        c[:, cc:cc + NX] = np.cos(ang)
        c[:, cs:cs + NX] = np.sin(ang)
    return c


def laid_out(i):
    a = {}

    def col(v):
        return np.asarray(v).reshape(-1, P).T

    a["x"] = i["x"][0]
    a["ctx"] = i["ctx"][0]
    a["ada_w"] = i["ada_w"]
    cc = np.stack([col(i["c"][0]), col(i["c_ctx"])], axis=2).reshape(P, 16)
    pos_head = [(p // 2) + 4 * (p % 2) for p in range(8)]
    a["vecs"] = np.concatenate([
        cc, col(i["ada_b"][0]), col(i["ada_b"][1]), col(i["norm_mix_g"][0]), col(i["norm_mix_g"][1]),
        col(i["norm_ffn_g"][0]), col(i["norm_ffn_g"][1]), col(i["hg_lb_logits"][0]), col(i["hg_lb_logits"][1]),
        col(i["hg_norm_g"][0]), col(i["ga_q_norm_g"][0]), col(i["ga_k_norm_g"][0]),
        np.broadcast_to(i["sw_sink"][0][pos_head], (P, 8))], axis=1)
    w = i["ab_w_in"][0]
    q0 = 5 * HG_W
    sq = [w[:, q0 + 64 * h:q0 + 64 * h + 64] for h in pos_head]
    feat = np.concatenate([w[:, 0:3 * HG_W], w[:, 4 * HG_W:5 * HG_W]] + sq + [w[:, q0 + 512:q0 + 640]], axis=1)
    a["wf0"] = feat.reshape(DC, P, FEAT0, P).transpose(2, 1, 0, 3).reshape(FEAT0, P, D)
    tok = np.concatenate([w[:, 3 * HG_W:4 * HG_W], w[:, q0 + 640:q0 + 768]], axis=1)
    a["wt0"] = tok.reshape(DC, P, TOK0).transpose(1, 0, 2).reshape(P, DC * TOK0)
    w = i["ga_w_in"][0]
    a["wf1"] = w[:, 0:10 * P].reshape(DC, P, FEAT1, P).transpose(2, 1, 0, 3).reshape(FEAT1, P, D)
    a["wt1"] = w[:, 10 * P:].reshape(DC, P, TOK1).transpose(1, 0, 2).reshape(P, DC * TOK1)
    wo = i["ab_w_out"][0]
    a["wo0"] = np.concatenate([wo[0:HG_W]] + [wo[HG_W + 64 * h:HG_W + 64 * h + 64] for h in pos_head], axis=0)
    a["wo1"] = i["ga_w_out"][0]
    for l in range(2):
        a[f"wq{l}"] = i["peer_w_q"][l]
        a[f"skT{l}"] = i["peer_sub_keys"][l].reshape(2 * PH, KEYS, P).transpose(0, 2, 1)
        a[f"uv{l}"] = np.concatenate([i["peer_u"][l], i["peer_v"][l]], axis=1)
    a["final_g"] = i["final_norm_g"]
    a["consts"] = shape_constants()
    return {k: np.ascontiguousarray(v) for k, v in a.items()}


def build(nc, arrays, phases=PHASES):
    dram = {k: nc.dram_tensor(f"in_{k}", v.shape, mybir.dt.from_np(v.dtype), kind="ExternalInput").ap()
            for k, v in arrays.items()}
    dram["out"] = nc.dram_tensor("out_y", (NX, D), F32, kind="ExternalOutput").ap()
    dram["modr"] = nc.dram_tensor("modr", (2, 2, 6 * D), F32, kind="Internal").ap()
    trunk(nc, dram, phases)


def kernel(**inputs):
    import concourse.bacc as bacc
    from concourse.bass_utils import run_bass_kernel_spmd

    arrays = laid_out({k: np.asarray(v) for k, v in inputs.items()})
    nc = bacc.Bacc("TRN2", target_bir_lowering=False, num_devices=1)
    build(nc, arrays)
    r = run_bass_kernel_spmd(nc, [{f"in_{k}": v for k, v in arrays.items()}], core_ids=[0])
    return r.results[0]["out_y"].reshape(1, NX, D)
```

```python
from contextlib import ExitStack

import numpy as np

import concourse.bass as bass
from concourse import mybir

P = 128
D = 1024
DC = D // P
NX, NCTX = 512, 256
T = NX + NCTX
NT = T // P
NTX = NX // P
EPS = 1e-6

HG_HEADS = 4
HG_W = 512
FEAT0 = 21
F_Q, F_FF, F_FB, F_G, F_SQ, F_SK = 0, 4, 8, 12, 16, 20
TOK0 = HG_W + 128
FEAT1 = 10
TOK1 = 256
LEVELS = 7
SPAN = [64 >> l for l in range(LEVELS)]
FORWARD, BACKWARD = 0, 1

RING = 8
KEYS = 128
EXPERTS = KEYS * KEYS
PH = 8
TOPK = 16
PICKS = PH * TOPK

C_ID, C_ROT_SW, C_ROT_GA = 0, 128, 256
C_WL, C_WR, C_IOTA = 384, 512, 640
C_HGM = 672
C_SW_COS, C_SW_SIN, C_GA_COS, C_GA_SIN = 1696, 2208, 2720, 3232
C_ALL = 3744

V_C, V_BIAS, V_GMIX, V_GFFN = 0, 16, 112, 128
V_LB, V_HGN, V_GAQ, V_GAK, V_SINK = 144, 152, 153, 154, 155
V_ALL = 163

ALU = mybir.AluOpType
ACT = mybir.ActivationFunctionType
F32 = mybir.dt.float32
F32R = mybir.dt.float32r
BF16 = mybir.dt.bfloat16
U32 = mybir.dt.uint32
AX = mybir.AxisListType.X


class Core:

    def __init__(self, nc, dram):
        self.nc = nc
        self.dram = dram
        self.phase = ""

    def opener(self, ctx, phase):
        self.phase = phase
        nc = self.nc
        taken = []

        def clear():
            nc.clear_and_free_semaphores(taken)
            nc.all_engine_barrier()

        ctx.callback(clear)

        def sb(name, shape, dt=F32):
            return ctx.enter_context(nc.sbuf_tensor(f"{phase}_{name}", shape, dt))

        def ps(name, shape, dt=F32):
            return ctx.enter_context(nc.psum_tensor(f"{phase}_{name}", shape, dt))

        def sem(name):
            taken.append(nc.alloc_semaphore(name=f"{phase}_{name}"))
            return taken[-1]

        return sb, ps, sem


def linker(engine, sem):
    count = [0]

    def link(instruction):
        count[0] += 1
        instruction.then_inc(sem, 1)
        engine.wait_ge(sem, count[0])

    return link


def wait_plain(engine, sem, value, passed):
    engine.wait_ge(sem, value)
    if not isinstance(value, int):
        engine.sem_inc(passed, 1)


def write_high(nc, high, x):
    return nc.vector.tensor_copy(high.bitcast(F32R), x)


def write_low(engine, low, x, high):
    return engine.tensor_tensor(low.bitcast(F32R), x, high, ALU.subtract)


MOD_GC = 256
MOD_MT = MOD_GC // P
MOD_GROUPS = 6 * D // MOD_GC
MOD_FIRST = 2 * D // MOD_GC
MOD_EARLY = [(0, g) for g in range(MOD_FIRST)]
MOD_LATE = [(0, g) for g in range(MOD_FIRST, MOD_GROUPS)] + [(1, g) for g in range(MOD_GROUPS)]


def add_bias(core, layer, lo, hi, sums):
    bias = core.vecs[:, V_BIAS + 48 * layer + lo:V_BIAS + 48 * layer + hi]
    return core.nc.vector.tensor_tensor(core.modc[:, layer, :, lo:hi].rearrange("p k m -> p m k"),
                                        sums.rearrange("p (m k) -> p m k", k=2),
                                        bias.unsqueeze(2).to_broadcast([P, hi - lo, 2]), ALU.add)


def apply_gain(core, layer, part):
    gain = (V_GMIX if part == 1 else V_GFFN) + 8 * layer
    for kind in range(2):
        v = core.modc[:, layer, kind, part * 8:part * 8 + 8]
        last = core.nc.vector.scalar_tensor_tensor(out=v, in0=v, scalar=1.0, in1=core.vecs[:, gain:gain + 8],
                                                   op0=ALU.add, op1=ALU.mult)
    return last


class Modulation:
    RING = 3
    POOL = 5

    def __init__(self, core, groups, sb, ps, sem):
        self.core = core
        self.groups = groups
        self.w = sb("ada", [P, self.RING, DC, MOD_GC])
        self.high = sb("adahigh", [P, 2, DC, MOD_GC])
        self.low = sb("adalow", [P, 2, DC, MOD_GC])
        self.line = sb("adaline", [4, MOD_GC])
        self.bank = ps("modsums", [P, 512])
        self.sums = self.bank[:, MOD_GC:MOD_GC + 2 * MOD_MT * len(groups)]
        self.s_w = [sem(f"ada{i}") for i in range(self.RING)]
        self.s_high, self.s_low_pool, self.s_low_dve = sem("ada_high"), sem("ada_low_pool"), sem("ada_low_dve")
        self.s_used, self.s_line, self.s_sums = sem("ada_used"), sem("ada_line"), sem("ada_sums")

    def load(self, sp):
        for n, (layer, g) in enumerate(self.groups):
            if n >= self.RING:
                sp.wait_ge(self.s_low_pool, n - self.RING + 1)
                sp.wait_ge(self.s_low_dve, n - self.RING + 1)
            src = self.core.dram["ada_w"][layer].rearrange("(c p) n -> p c n", p=P)
            sp.dma_start(self.w[:, n % self.RING], src[:, :, g * MOD_GC:(g + 1) * MOD_GC]).then_inc(
                self.s_w[n % self.RING], 16)

    def split(self, dve, n):
        w, high, low = self.w[:, n % self.RING], self.high[:, n % 2], self.low[:, n % 2]
        dve.wait_ge(self.s_w[n % self.RING], 16 * (n // self.RING + 1))
        if n >= 2:
            dve.wait_ge(self.s_used, n - 1)
        write_high(self.core.nc, high, w).then_inc(self.s_high, 1)
        dve.wait_ge(self.s_high, n + 1)
        write_low(self.core.nc.vector, low[:, self.POOL:], w[:, self.POOL:], high[:, self.POOL:]).then_inc(
            self.s_low_dve, 1)

    def split_pool(self, pool, n):
        w, high, low = self.w[:, n % self.RING], self.high[:, n % 2], self.low[:, n % 2]
        pool.wait_ge(self.s_high, n + 1)
        write_low(self.core.nc.gpsimd, low[:, 0:self.POOL], w[:, 0:self.POOL], high[:, 0:self.POOL]).then_inc(
            self.s_low_pool, 1)

    def multiply(self, pe, n):
        pe.wait_ge(self.s_low_pool, n + 1)
        pe.wait_ge(self.s_low_dve, n + 1)
        if n >= 1:
            pe.wait_ge(self.s_line, n)
        halves = (self.high[:, n % 2], self.low[:, n % 2])
        for x, half in enumerate(halves):
            for c in range(DC):
                last = self.core.nc.tensor.matmul(self.bank[0:4, 0:MOD_GC], self.core.silu[:, c, :].bitcast(F32R),
                                                  half[:, c, :].bitcast(F32R), start=(x == 0 and c == 0),
                                                  stop=(x == 1 and c == DC - 1))
        last.then_inc(self.s_used, 1)

    def copy_line(self, dve, n):
        dve.wait_ge(self.s_used, n + 1)
        if n >= 1:
            dve.wait_ge(self.s_sums, n)
        self.core.nc.vector.tensor_copy(self.line[:], self.bank[0:4, 0:MOD_GC]).then_inc(self.s_line, 1)

    def turn(self, pe, n):
        pe.wait_ge(self.s_line, n + 1)
        for m in range(MOD_MT):
            at = 2 * (MOD_MT * n + m)
            last = self.core.nc.tensor.matmul(self.sums[:, at:at + 2], self.line[:, m * P:(m + 1) * P],
                                              self.core.pairs[:], start=True, stop=True)
        last.then_inc(self.s_sums, 1)


def modulation(core):
    nc = core.nc
    with ExitStack() as ctx:
        sb, ps, sem = core.opener(ctx, "mod")
        tmp = sb("tmp", [P, DC, 2])
        silu = sb("silu_c", [P, DC, 2])
        lbw = sb("lbw", [P, 12])
        mod = Modulation(core, MOD_EARLY, sb, ps, sem)
        square = sb("square", [P, D])
        ssq = sb("ssq", [P, NT])
        s_const, s_silu, s_link, s_exp, s_lb = sem("const"), sem("silu"), sem("link"), sem("exp"), sem("lb")
        s_x, s_ssq, s_std = [sem(f"x{i}") for i in range(NT)], sem("ssq"), sem("std")
        block = ctx.enter_context(nc.Block())

        @block.sync
        def _(sp):
            sp.dma_start(core.vecs[:], core.dram["vecs"]).then_inc(s_const, 16)
            sp.dma_start(core.ident[:], core.dram["consts"][:, C_ID:C_ID + P]).then_inc(s_const, 16)
            mod.load(sp)

        @block.gpsimd
        def _(pool):
            for n in range(len(MOD_EARLY)):
                mod.split_pool(pool, n)

        @block.tensor
        def _(pe):
            pe.wait_ge(s_silu, 1)
            for n in range(len(MOD_EARLY)):
                mod.multiply(pe, n)
                mod.turn(pe, n)

        @block.scalar
        def _(act):
            for i in range(NT):
                src = core.dram["x"][i * P:(i + 1) * P, :] if i < NTX else core.dram["ctx"][(i - NTX) * P:(i - NTX + 1) * P, :]
                act.dma_start(core.h[:, i, :], src).then_inc(s_x[i], 16)
            act.wait_ge(s_const, 32)
            nc.scalar.activation(tmp[:].rearrange("p c k -> p (c k)"), core.vecs[:, V_C:V_C + 16],
                                 ACT.Exp, scale=-1.0).then_inc(s_exp, 1)
            act.wait_ge(s_lb, 1)
            nc.scalar.activation(lbw[:, 0:8], lbw[:, 0:8], ACT.Exp).then_inc(s_exp, 1)
            for i in range(NT):
                act.wait_ge(s_x[i], 16)
                if i > 0:
                    act.wait_ge(s_ssq, i)
                nc.scalar.activation(square[:], core.h[:, i, :], ACT.Square, accum_out=ssq[:, i:i + 1]).then_inc(s_ssq, 1)
                act.wait_ge(s_ssq, i + 1)
                nc.scalar.activation(ssq[:, i:i + 1], ssq[:, i:i + 1], ACT.Sqrt, scale=1.0 / D,
                                     bias=core.eps[:]).then_inc(s_std, 1)

        @block.vector
        def _(dve):
            link = linker(dve, s_link)
            lbl = core.vecs[:, V_LB:V_LB + 8]
            dve.wait_ge(s_const, 32)
            nc.vector.memset(core.ones[:], 1.0)
            nc.vector.memset(core.eps[:], EPS)
            nc.vector.tensor_tensor(core.pairs[:], core.ident[0:4, 0:2], core.ident[0:4, 2:4], ALU.add)
            link(nc.vector.tensor_tensor(lbw[:, 8:12], lbl[:, 0:4], lbl[:, 4:8], ALU.max))
            link(nc.vector.tensor_tensor(lbw[:, 0:4], lbl[:, 0:4], lbw[:, 8:12], ALU.subtract))
            nc.vector.tensor_tensor(lbw[:, 4:8], lbl[:, 4:8], lbw[:, 8:12], ALU.subtract).then_inc(s_lb, 1)
            t2 = tmp[:].rearrange("p c k -> p (c k)")
            dve.wait_ge(s_exp, 1)
            link(nc.vector.tensor_scalar(t2, t2, 1.0, None, ALU.add))
            link(nc.vector.reciprocal(t2, t2))
            link(nc.vector.tensor_tensor(silu[:].rearrange("p c k -> p (c k)"), t2, core.vecs[:, V_C:V_C + 16],
                                         ALU.mult))
            link(write_high(nc, core.silu[:, :, 0:2], silu[:]))
            write_low(nc.vector, core.silu[:, :, 2:4], silu[:], core.silu[:, :, 0:2]).then_inc(s_silu, 1)
            dve.wait_ge(s_exp, 2)
            link(nc.vector.tensor_tensor(lbw[:, 8:12], lbw[:, 0:4], lbw[:, 4:8], ALU.add))
            link(nc.vector.reciprocal(lbw[:, 8:12], lbw[:, 8:12]))
            link(nc.vector.tensor_tensor(core.lb[:, 0:4], lbw[:, 0:4], lbw[:, 8:12], ALU.mult))
            link(nc.vector.tensor_scalar(core.lb[:, 4:8], core.lb[:, 0:4], -1.0, 1.0, ALU.mult, ALU.add))
            count = len(MOD_EARLY)
            for n in range(count + 1):
                if n < count:
                    mod.split(dve, n)
                if n > 0:
                    mod.copy_line(dve, n - 1)
                i = n - (count + 1 - NT)
                if i >= 0:
                    dve.wait_ge(s_std, i + 1)
                    link(nc.vector.reciprocal(ssq[:, i:i + 1], ssq[:, i:i + 1]))
                    link(nc.vector.tensor_scalar(core.h[:, i, :], core.h[:, i, :], ssq[:, i:i + 1], None, ALU.mult))
            dve.wait_ge(mod.s_sums, count)
            link(add_bias(core, 0, 0, MOD_MT * MOD_FIRST, mod.sums))
            link(apply_gain(core, 0, 1))


class LateModulation(Modulation):

    def __init__(self, core, sb, ps, sem):
        super().__init__(core, MOD_LATE, sb, ps, sem)
        self.rows = sb("modrows", [96, 2, P])
        self.s_modc, self.s_turned = sem("modc"), sem("turned")
        self.s_rows, self.s_out = sem("modrows_made"), sem("modrows_out")

    def store(self, sp):
        for layer in range(2):
            sp.wait_ge(self.s_rows, layer + 1)
            sp.dma_start(self.core.dram["modr"][layer].rearrange("k (r q) -> (k r) q", q=P),
                         self.rows[:, layer, :]).then_inc(self.s_out, 16)
        sp.wait_ge(self.s_out, 32)

    def finish(self, dve, link):
        core = self.core
        late0 = 2 * MOD_MT * (MOD_GROUPS - MOD_FIRST)
        dve.wait_ge(self.s_sums, len(MOD_LATE))
        link(add_bias(core, 0, MOD_MT * MOD_FIRST, 48, self.sums[:, 0:late0]))
        link(add_bias(core, 1, 0, 48, self.sums[:, late0:]))
        apply_gain(core, 0, 4)
        apply_gain(core, 1, 1)
        apply_gain(core, 1, 4).then_inc(self.s_modc, 1)

    def turn_rows(self, pe):
        pe.wait_ge(self.s_modc, 1)
        for layer in range(2):
            last = self.core.nc.tensor.transpose(self.bank[0:96, layer * P:(layer + 1) * P],
                                                 self.core.modc[:, layer].rearrange("p k m -> p (k m)"),
                                                 self.core.ident[:])
        last.then_inc(self.s_turned, 1)

    def move_rows(self, dve):
        dve.wait_ge(self.s_turned, 1)
        for layer in range(2):
            self.core.nc.vector.tensor_copy(self.rows[:, layer, :],
                                            self.bank[0:96, layer * P:(layer + 1) * P]).then_inc(self.s_rows, 1)


def project(core, layer, feat, featT, tokV, ntok_cols, q_tiles, sums=None):
    nc = core.nc
    WR = 2
    VALUES = ntok_cols // P
    UNITS = feat + VALUES
    GATED = 16 if sums is not None else 0
    rest = list(range(feat, UNITS)) + list(range(GATED, feat))
    order = []
    for m in range(GATED):
        order.append(m)
        if m % 2 and rest:
            order.append(rest.pop(0))
    order += rest
    gated = [m for m in order if m < GATED]
    blocks = [n for n, m in enumerate(order) if m >= feat]
    with ExitStack() as ctx:
        sb, ps, sem = core.opener(ctx, f"proj{layer}")
        h = core.h
        aH = sb("aH", [P, DC, T])
        aL = sb("aL", [P, DC, T])
        wf = sb("wf", [P, WR, DC, P])
        wH = sb("wH", [P, WR, DC, P])
        wL = sb("wL", [P, WR, DC, P])
        if layer == 0:
            aT = tokV[:].rearrange("p i n -> p (i n)")[:, 0:2 * D].rearrange("p (a c t) -> p a c t", a=2, t=P)
        else:
            aT = sb("aT", [P, 2, DC, P])[:]
        xn = featT[:, feat - 3:feat, :].rearrange("p m t -> p (m t)")[:, 0:2 * D].rearrange("p (a d) -> p a d", a=2)
        ssq = sb("ssq", [P, NT])
        rstd = sb("rstd", [P, NT])
        pt = ps("pt", [P, 4, 512])
        pf = ps("pf", [P, 2, 2, 512])
        s_wf = [sem(f"wf{i}") for i in range(WR)]
        s_aH, s_aL, s_wH, s_wL = sem("aH"), sem("aL"), sem("wH"), sem("wL")
        s_ssq, s_std, s_link, s_xn = sem("ssq"), sem("std"), sem("link"), sem("xn")
        s_tr, s_aT, s_f, s_fe = sem("tr"), sem("aT"), sem("f"), [sem("fe_even"), sem("fe_odd")]
        s_bounded, s_exp, s_forget, s_logf = (sem(n) for n in ("bounded", "exp", "forget", "logf"))
        spare = h[:].rearrange("p i d -> p (i d)")
        work = spare[:, 0:4 * T].rearrange("p (a b t) -> p a b t", a=2, b=2)
        vT = spare[:, 4 * T:6 * T].rearrange("p (a t) -> p a t", a=2) if layer == 0 else sb("vT", [P, 2, T])[:]
        s_turned, s_values = sem("turned"), sem("values")
        block = ctx.enter_context(nc.Block())
        wfd, wtd = core.dram[f"wf{layer}"], core.dram[f"wt{layer}"]

        def groups(tile):
            return range(tile * 4, tile * 4 + 4)

        def evacuate(eng, i):
            kind = 0 if i < NTX else 1
            if i >= 2:
                eng.wait_ge(s_aL, i - 1)
            for g in groups(i):
                eng.wait_ge(s_tr, g + 1)
                for c2 in range(2):
                    c = 2 * (g % 4) + c2
                    last = nc.scalar.activation(aT[:, i % 2, c, :], pt[:, g % 4, c2 * P:(c2 + 1) * P],
                                                ACT.Identity, scale=core.modc[:, layer, kind, 8 + c:9 + c],
                                                bias=core.modc[:, layer, kind, c:c + 1])
                last.then_inc(s_aT, 1)

        def width(m):
            return NX if m < q_tiles else T

        def is_forget(m):
            return F_FF <= m < F_G

        forgets = [m for m in range(GATED) if is_forget(m)]

        def turned_back(v):
            return pt[:, 2 * (v % 2):2 * (v % 2) + 2].rearrange("p a n -> p (a n)")[:, 0:T]

        @block.sync
        def _(sp):
            values = wtd.rearrange("p (c n) -> p c n", c=DC)
            for n, m in enumerate(order):
                if n >= WR:
                    sp.wait_ge(s_wL, n - WR + 1)
                if m < feat:
                    src = wfd[m].rearrange("p (c n) -> p c n", c=DC)
                else:
                    src = values[:, :, (m - feat) * P:(m - feat + 1) * P]
                sp.dma_start(wf[:, n % WR], src).then_inc(s_wf[n % WR], 16)

        @block.gpsimd
        def _(pool):
            def low_tokens(i):
                pool.wait_ge(s_aH, i + 1)
                cols = slice(i * P, (i + 1) * P)
                write_low(nc.gpsimd, aL[:, :, cols], aT[:, i % 2], aH[:, :, cols]).then_inc(s_aL, 1)

            def low_weights(m):
                pool.wait_ge(s_wH, m + 1)
                write_low(nc.gpsimd, wL[:, m % WR], wf[:, m % WR], wH[:, m % WR]).then_inc(s_wL, 1)

            for i in range(NT):
                low_tokens(i)
            for m in range(UNITS):
                low_weights(m)

        @block.scalar
        def _(act):
            for i in range(NT):
                if layer == 0:
                    evacuate(act, i)
                    continue
                if i >= 2:
                    act.wait_ge(s_tr, 4 * (i - 1))
                nc.scalar.activation(xn[:, i % 2, :], h[:, i, :], ACT.Square,
                                     accum_out=ssq[:, i:i + 1]).then_inc(s_ssq, 1)
                act.wait_ge(s_ssq, i + 1)
                nc.scalar.activation(rstd[:, i:i + 1], ssq[:, i:i + 1], ACT.Sqrt, scale=1.0 / D,
                                     bias=core.eps[:]).then_inc(s_std, 1)
                if i >= 2:
                    evacuate(act, i - 2)
            if layer > 0:
                evacuate(act, NT - 2)
                evacuate(act, NT - 1)

            def move_unit(n):
                m = order[n]
                act.wait_ge(s_f, n + 1)
                src = pf[:, n % 2].rearrange("p a n -> p (a n)")[:, 0:width(m)]
                if m >= feat:
                    v = m - feat
                    if v >= 2:
                        act.wait_ge(s_turned, v - 1)
                    dst = vT[:, v % 2, :]
                else:
                    dst = featT[:, m, 0:width(m)]
                nc.scalar.activation(dst, src, ACT.Copy).then_inc(s_fe[n % 2], 1)

            def move_values(v):
                act.wait_ge(s_turned, v + 1)
                nc.scalar.activation(tokV[:, :, v * P:(v + 1) * P],
                                     turned_back(v).rearrange("p (i n) -> p i n", n=P), ACT.Copy).then_inc(s_values, 1)

            def log_forget(j):
                if 0 <= j < GATED and gated[j] in forgets:
                    act.wait_ge(s_forget, forgets.index(gated[j]) + 1)
                    nc.scalar.activation(work[:, 1, j % 2], work[:, 1, j % 2], ACT.Ln).then_inc(s_logf, 1)

            for n, m in enumerate(order):
                move_unit(n)
                if m < GATED:
                    act.wait_ge(s_bounded, m + 1)
                    nc.scalar.activation(work[:, 0, m % 2], work[:, 0, m % 2], ACT.Exp, scale=-1.0).then_inc(s_exp, 1)
                    log_forget(m - 1)
                if n - 1 in blocks:
                    move_values(blocks.index(n - 1))

        @block.vector
        def _(dve):
            link = linker(dve, s_link)

            def high_tokens(i):
                dve.wait_ge(s_aT, 4 * (i + 1))
                cols = slice(i * P, (i + 1) * P)
                write_high(nc, aH[:, :, cols], aT[:, i % 2]).then_inc(s_aH, 1)

            def high_weights(n):
                if n < UNITS:
                    dve.wait_ge(s_wf[n % WR], 16 * (n // WR + 1))
                    if n >= WR:
                        dve.wait_ge(s_f, n - WR + 1)
                    write_high(nc, wH[:, n % WR], wf[:, n % WR]).then_inc(s_wH, 1)

            for i in range(NT):
                if layer == 0:
                    if i == 3:
                        high_weights(0)
                        high_weights(1)
                    high_tokens(i)
                    continue
                dve.wait_ge(s_std, i + 1)
                link(nc.vector.reciprocal(rstd[:, i:i + 1], rstd[:, i:i + 1]))
                if i >= 2:
                    dve.wait_ge(s_tr, 4 * (i - 1))
                nc.vector.tensor_scalar(xn[:, i % 2, :], h[:, i, :], rstd[:, i:i + 1], None,
                                        ALU.mult).then_inc(s_xn, 1)
                if i >= 1:
                    high_tokens(i - 1)
            if layer > 0:
                high_weights(0)
                high_tokens(NT - 1)
                high_weights(1)

            def bound(m):
                n = order.index(m)
                dve.wait_ge(s_fe[n % 2], n // 2 + 1)
                nc.vector.tensor_scalar(work[:, 0, m % 2], featT[:, m, :], -40.0 if is_forget(m) else -80.0, None,
                                        ALU.max).then_inc(s_bounded, 1)

            def gate(m):
                e, r = work[:, 0, m % 2], work[:, 1, m % 2]
                dve.wait_ge(s_exp, m + 1)
                link(nc.vector.tensor_scalar(r, e, 1.0, None, ALU.add))
                link(nc.vector.reciprocal(r, r))
                if is_forget(m):
                    hd = (m - F_FF) % HG_HEADS
                    lb, omlb = core.lb[:, hd:hd + 1], core.lb[:, 4 + hd:5 + hd]
                    link(nc.vector.scalar_tensor_tensor(out=featT[:, m, :], in0=e, scalar=omlb, in1=r,
                                                        op0=ALU.mult, op1=ALU.mult))
                    nc.vector.tensor_scalar(r, r, omlb, lb, ALU.mult, ALU.add).then_inc(s_forget, 1)
                else:
                    link(nc.vector.tensor_tensor(featT[:, m, :], featT[:, m, :], r, ALU.mult))

            def running_sums(m):
                if m in forgets:
                    dve.wait_ge(s_logf, forgets.index(m) + 1)
                    for s in range(NT):
                        last = nc.vector.tensor_tensor_scan(sums[:, m - F_FF, s, 1:P + 1], core.ones[:],
                                                            work[:, 1, m % 2, s * P:(s + 1) * P], 0.0,
                                                            ALU.mult, ALU.add)
                    link(last)

            if GATED:
                dve.wait_ge(s_tr, 4 * NT)
                nc.vector.memset(sums[:, :, :, 0], 0.0)
            for n, m in enumerate(order):
                high_weights(n + 2)
                if m < GATED:
                    bound(m)
                    gate(m)
                    running_sums(m - 1)

        @block.tensor
        def _(pe):
            for i in range(NT):
                if layer > 0:
                    pe.wait_ge(s_xn, i + 1)
                for g in groups(i):
                    if g >= 4:
                        pe.wait_ge(s_aT, g - 3)
                    for c2 in range(2):
                        c = 2 * (g % 4) + c2
                        last = nc.tensor.transpose(pt[:, g % 4, c2 * P:(c2 + 1) * P],
                                                   (h[:, i] if layer == 0 else xn[:, i % 2])[:, c * P:(c + 1) * P],
                                                   core.ident[:])
                    last.then_inc(s_tr, 1)
            pe.wait_ge(s_aL, NT)

            def three_passes(out, left, right):
                for x, y in ((0, 0), (0, 1), (1, 0)):
                    for c in range(DC):
                        last = nc.tensor.matmul(out, left(x, c).bitcast(F32R), right(y, c).bitcast(F32R),
                                                start=(x == 0 and y == 0 and c == 0), stop=(x == 1 and c == DC - 1))
                return last

            def turn_values(v):
                n = blocks[v]
                pe.wait_ge(s_fe[n % 2], n // 2 + 1)
                if v >= 2:
                    pe.wait_ge(s_values, v - 1)
                for i in range(NT):
                    last = nc.tensor.transpose(turned_back(v)[:, i * P:(i + 1) * P], vT[:, v % 2, i * P:(i + 1) * P],
                                               core.ident[:])
                last.then_inc(s_turned, 1)

            for n, m in enumerate(order):
                weights, tokens = (wH[:, n % WR], wL[:, n % WR]), (aH, aL)
                pe.wait_ge(s_wL, n + 1)
                if n >= 2:
                    pe.wait_ge(s_fe[n % 2], n // 2)
                for lo, hi in ((0, NX), (NX, T)):
                    if lo < width(m):
                        last = three_passes(pf[:, n % 2, lo // NX, 0:hi - lo], lambda x, c: weights[x][:, c, :],
                                            lambda y, c: tokens[y][:, c, lo:hi])
                last.then_inc(s_f, 1)
                if n - 1 in blocks:
                    turn_values(blocks.index(n - 1))


def hgrn(core, featT, tokV, C):
    nc = core.nc
    NCH = T // P
    ORDER = {FORWARD: [4, 5, 0, 1, 2, 3], BACKWARD: [5, 4, 3, 2, 1, 0]}
    UC = 3
    UW = UC * P
    NB = 10
    BATCHES = [(0, 4), (4, 8), (8, 10)]
    with ExitStack() as ctx:
        sb, ps, sem = core.opener(ctx, "hgrn")
        hspace = core.h[:].rearrange("p i d -> p (i d)")
        state = hspace[:, 0:3072].rearrange("p (b r n v) -> p b r n v", b=2, r=2, n=6)
        qe = hspace[:, 3072:6144].rearrange("p (b r t) -> p b r t", b=2, r=2)
        ke = sb("ke", [P, 2, T])
        kq = sb("kq", [P, 2, 2, LEVELS, UW])
        diff = sb("diff", [P, 4, UW])
        pm = sb("pm", [P, 2, 1024])
        keT = sb("keT", [P, 4, P])
        decay = sb("decay", [P, 2, 2, NCH])
        mask = sb("mask", [P, 1024])
        pP = ps("pP", [P, 2, 1024])
        pO = ps("pO", [P, 2, 512])
        pTr = ps("pTr", [P, 4, P])
        pKV = ps("pKV", [P, 4, P])
        names = ("mask", "link", "sum", "scaled", "kqe", "tr", "trv", "kv", "state", "sub", "lexp", "kq", "P", "pm",
                 "O", "oT", "sq", "ms", "log", "std")
        S = {n: sem(n) for n in names}
        block = ctx.enter_context(nc.Block())
        flat = kq[:].rearrange("p a b l t -> p (a b l t)")

        def keys(hd, r):
            return featT[:, (F_FF, F_FB)[r] + hd, :]

        def inverse(hd):
            return flat[:, 3072 + hd * T:3072 + (hd + 1) * T]

        def chunked(x):
            return x.rearrange("p (n t) -> p n t", t=P)

        def level_views(hd, u, r, l):
            m = SPAN[l]
            nb = P // (2 * m)
            first = 1 if r == FORWARD else 0
            c = C[:, HG_HEADS * r + hd, u * UC:(u + 1) * UC, :]
            at = c[:, :, first:first + P].rearrange("p n (b w) -> p n b w", w=2 * m)
            cut = c[:, :, m:P:2 * m].unsqueeze(3).to_broadcast([P, UC, nb, 2 * m])
            return at, cut

        def halves(x, u, m):
            v = x[:, u * UW:(u + 1) * UW].rearrange("p (b w) -> p b w", w=2 * m)
            return v[:, :, 0:m], v[:, :, m:2 * m]

        @block.sync
        def _(sp):
            sp.dma_start(mask[:], core.dram["consts"][:, C_HGM:C_HGM + 1024]).then_inc(S["mask"], 16)

        @block.gpsimd
        def _(pool):
            n = 0
            for hd in range(HG_HEADS):
                for u in range(2):
                    for l in range(LEVELS):
                        for r in range(2):
                            at, cut = level_views(hd, u, r, l)
                            o = diff[:, n % 4, :].rearrange("p (n b w) -> p n b w", n=UC, w=2 * SPAN[l])
                            if n >= 4:
                                pool.wait_ge(S["lexp"], n - 3)
                            nc.gpsimd.tensor_tensor(o, at, cut, ALU.subtract).then_inc(S["sub"], 1)
                            n += 1

        @block.scalar
        def _(act):
            def exp_sums(hd):
                hb = hd % 2
                act.wait_ge(S["sum"], hd + 1)
                last = nc.scalar.activation(ke[:, FORWARD], ke[:, FORWARD], ACT.Exp)
                last = nc.scalar.activation(qe[:, hb, BACKWARD], qe[:, hb, BACKWARD], ACT.Exp)
                last = nc.scalar.activation(chunked(ke[:, BACKWARD]), C[:, HG_HEADS + hd, :, 0:P], ACT.Exp)
                last = nc.scalar.activation(chunked(qe[:, hb, FORWARD]), C[:, hd, :, 1:P + 1], ACT.Exp)
                last = nc.scalar.activation(decay[:, hb], C[:, hd:hd + HG_HEADS + 1:HG_HEADS, :, P], ACT.Exp)
                last.then_inc(S["scaled"], 1)

            def move_keys(hd):
                for g, (lo, hi) in enumerate(BATCHES):
                    n = hd * len(BATCHES) + g
                    act.wait_ge(S["tr"], n + 1)
                    if n > 0:
                        act.wait_ge(S["kv"], n)
                    nc.scalar.activation(keT[:, 0:hi - lo, :], pTr[:, 0:hi - lo, :], ACT.Copy).then_inc(S["trv"], 1)

            def exp_levels(hd, u, levels=range(LEVELS)):
                if hd > 0 and levels[0] == 0:
                    act.wait_ge(S["P"], (hd - 1) * NCH + (u + 1) * UC)
                for l in levels:
                    m = SPAN[l]
                    keys, queries = (halves(kq[:, u, x, l, :], 0, m) for x in range(2))
                    for r in range(2):
                        n = ((hd * 2 + u) * LEVELS + l) * 2 + r
                        left, right = halves(diff[:, n % 4, :], 0, m)
                        to_left, to_right = (keys[0], queries[1]) if r == FORWARD else (queries[0], keys[1])
                        act.wait_ge(S["sub"], n + 1)
                        nc.scalar.activation(to_left, left, ACT.Exp, scale=-1.0)
                        nc.scalar.activation(to_right, right, ACT.Exp).then_inc(S["lexp"], 1)

            def move_out(n):
                hd, s = divmod(n, NCH)
                act.wait_ge(S["O"], n + 1)
                nc.scalar.activation(featT[:, F_FF + hd, s * P:(s + 1) * P], pO[:, n % 2, 0:P],
                                     ACT.Copy).then_inc(S["oT"], 1)

            exp_sums(0)
            move_keys(0)
            exp_levels(0, 0)
            exp_levels(0, 1)
            for hd in range(HG_HEADS):
                more = hd + 1 < HG_HEADS
                n = hd * NCH
                move_out(n)
                move_out(n + 1)
                if more:
                    exp_sums(hd + 1)
                    exp_levels(hd + 1, 0, range(0, 3))
                move_out(n + 2)
                if more:
                    exp_levels(hd + 1, 0, range(3, 5))
                move_out(n + 3)
                if more:
                    exp_levels(hd + 1, 0, range(5, LEVELS))
                move_out(n + 4)
                if more:
                    move_keys(hd + 1)
                    exp_levels(hd + 1, 1, range(0, 4))
                move_out(n + 5)
                if more:
                    exp_levels(hd + 1, 1, range(4, LEVELS))
            for hd in range(HG_HEADS):
                act.wait_ge(S["oT"], HG_HEADS * NCH)
                nc.scalar.activation(flat[:, hd * T:(hd + 1) * T], featT[:, F_FF + hd, :],
                                     ACT.Square).then_inc(S["sq"], 1)
            for hd in range(HG_HEADS):
                act.wait_ge(S["ms"], hd + 1)
                nc.scalar.activation(inverse(hd), pP[:, hd % 2, 0:T], ACT.Ln, scale=1.0 / P,
                                     bias=core.eps[:]).then_inc(S["log"], 1)
            for hd in range(HG_HEADS):
                act.wait_ge(S["log"], hd + 1)
                nc.scalar.activation(inverse(hd), inverse(hd), ACT.Exp, scale=-0.5).then_inc(S["std"], 1)

        @block.vector
        def _(dve):
            link = linker(dve, S["link"])

            def head_sums(hd):
                hb = hd % 2
                if hd > 0:
                    dve.wait_ge(S["tr"], len(BATCHES) * hd)
                if hd > 1:
                    dve.wait_ge(S["O"], (hd - 1) * NCH)
                fwd, bwd = C[:, hd], C[:, HG_HEADS + hd]
                nc.vector.tensor_tensor(chunked(ke[:, FORWARD]), fwd[:, :, P:P + 1].to_broadcast([P, NCH, P]),
                                        fwd[:, :, 1:P + 1], ALU.subtract)
                nc.vector.tensor_tensor(chunked(qe[:, hb, BACKWARD]), bwd[:, :, P:P + 1].to_broadcast([P, NCH, P]),
                                        bwd[:, :, 0:P], ALU.subtract).then_inc(S["sum"], 1)

            def scale_ends(hd):
                hb = hd % 2
                q = featT[:, F_Q + hd, :].unsqueeze(1).to_broadcast([P, 2, T])
                dve.wait_ge(S["scaled"], hd + 1)
                nc.vector.tensor_tensor(qe[:, hb], qe[:, hb], q, ALU.mult)
                nc.vector.tensor_tensor(ke[:], ke[:], featT[:, F_FF + hd:F_FB + hd + 1:HG_HEADS, :], ALU.mult).then_inc(S["kqe"], 1)

            def carry_states(hd):
                hb = hd % 2
                for b in range(NB):
                    r, n = divmod(b, NB // 2)
                    dve.wait_ge(S["kv"], hd * len(BATCHES) + b // 4 + 1)
                    if n == 0:
                        ins = nc.vector.tensor_copy(state[:, hb, r, 1, :], pKV[:, b % 4, :])
                    else:
                        dve.wait_ge(S["state"], hd * NB + b)
                        ins = nc.vector.scalar_tensor_tensor(
                            out=state[:, hb, r, n + 1, :], in0=state[:, hb, r, n, :],
                            scalar=decay[:, hb, r, ORDER[r][n]:ORDER[r][n] + 1],
                            in1=pKV[:, b % 4, :], op0=ALU.mult, op1=ALU.add)
                    ins.then_inc(S["state"], 1)

            def scale_levels(hd, u, levels):
                q = featT[:, F_Q + hd, u * UW:(u + 1) * UW]
                for l in levels:
                    m = SPAN[l]
                    left, right = halves(kq[:, u, 0, l, :], 0, m)
                    dve.wait_ge(S["lexp"], ((hd * 2 + u) * LEVELS + l) * 2 + 2)
                    nc.vector.tensor_tensor(kq[:, u, 1, l, :], kq[:, u, 1, l, :], q, ALU.mult)
                    nc.vector.tensor_tensor(left, left, halves(keys(hd, FORWARD), u, m)[0], ALU.mult)
                    nc.vector.tensor_tensor(right, right, halves(keys(hd, BACKWARD), u, m)[1],
                                            ALU.mult).then_inc(S["kq"], 1)

            def mask_pairs(n):
                dve.wait_ge(S["P"], n + 1)
                if n >= 2:
                    dve.wait_ge(S["O"], n - 1)
                nc.vector.tensor_tensor(pm[:, n % 2], pP[:, n % 2], mask[:], ALU.mult).then_inc(S["pm"], 1)

            head_sums(0)
            scale_ends(0)
            carry_states(0)
            dve.wait_ge(S["mask"], 16)
            scale_levels(0, 0, range(LEVELS))
            scale_levels(0, 1, range(0, 4))
            for hd in range(HG_HEADS):
                more = hd + 1 < HG_HEADS
                n = hd * NCH
                mask_pairs(n)
                scale_levels(hd, 1, range(4, LEVELS))
                mask_pairs(n + 1)
                mask_pairs(n + 2)
                if more:
                    head_sums(hd + 1)
                mask_pairs(n + 3)
                if more:
                    scale_ends(hd + 1)
                    scale_levels(hd + 1, 0, range(0, 3))
                mask_pairs(n + 4)
                if more:
                    scale_levels(hd + 1, 0, range(3, LEVELS))
                mask_pairs(n + 5)
                if more:
                    carry_states(hd + 1)
                    scale_levels(hd + 1, 1, range(0, 4))
            for hd in range(HG_HEADS):
                o = featT[:, F_FF + hd, :]
                std = inverse(hd)
                dve.wait_ge(S["std"], hd + 1)
                link(nc.vector.scalar_tensor_tensor(out=o, in0=o, scalar=core.vecs[:, V_HGN:V_HGN + 1], in1=std,
                                                    op0=ALU.mult, op1=ALU.mult))
                link(nc.vector.tensor_tensor(o, o, featT[:, F_G + hd, :], ALU.mult))

        @block.tensor
        def _(pe):
            def pairs(n):
                hd, s = divmod(n, NCH)
                u, c = s // UC, s % UC
                if n >= 2:
                    pe.wait_ge(S["pm"], n - 1)
                pe.wait_ge(S["kq"], (hd * 2 + u + 1) * LEVELS)
                q = featT[:, F_Q + hd, s * P:(s + 1) * P]
                for l in range(LEVELS):
                    x = kq[:, u, :, l, c * P:(c + 1) * P]
                    nc.tensor.matmul(pP[:, n % 2, P * l:P * l + P], x[:, 0, :], x[:, 1, :], start=True, stop=True)
                for r in range(2):
                    last = nc.tensor.matmul(pP[:, n % 2, P * LEVELS:P * LEVELS + P], keys(hd, r)[:, s * P:(s + 1) * P], q,
                                            start=(r == 0), stop=(r == 1))
                last.then_inc(S["P"], 1)

            def outputs(n):
                hd, s = divmod(n, NCH)
                hb = hd % 2
                o = pO[:, n % 2, 0:P]
                v = tokV[:, s, hd * P:(hd + 1) * P]
                pe.wait_ge(S["pm"], n + 1)
                pe.wait_ge(S["state"], (hd + 1) * NB)
                if n >= 2:
                    pe.wait_ge(S["oT"], n - 1)
                start = True
                for r in range(2):
                    at = ORDER[r].index(s)
                    if at > 0:
                        nc.tensor.matmul(o, state[:, hb, r, at, :], qe[:, hb, r, s * P:(s + 1) * P],
                                         start=start, stop=False)
                        start = False
                for l in range(LEVELS + 1):
                    last = nc.tensor.matmul(o, v, pm[:, n % 2, P * l:P * l + P], start=False, stop=(l == LEVELS))
                last.then_inc(S["O"], 1)

            def chunk_states(hd):
                pe.wait_ge(S["kqe"], hd + 1)
                for g, (lo, hi) in enumerate(BATCHES):
                    n = hd * len(BATCHES) + g
                    if n > 0:
                        pe.wait_ge(S["trv"], n)
                    for b in range(lo, hi):
                        r, at = divmod(b, NB // 2)
                        s = ORDER[r][at]
                        last = nc.tensor.transpose(pTr[:, b - lo, :], ke[:, r, s * P:(s + 1) * P], core.ident[:])
                    last.then_inc(S["tr"], 1)
                    pe.wait_ge(S["trv"], n + 1)
                    if n > 0:
                        pe.wait_ge(S["state"], hd * NB + lo)
                    for b in range(lo, hi):
                        r, at = divmod(b, NB // 2)
                        s = ORDER[r][at]
                        last = nc.tensor.matmul(pKV[:, b - lo, :], keT[:, b - lo, :],
                                                tokV[:, s, hd * P:(hd + 1) * P], start=True, stop=True)
                    last.then_inc(S["kv"], 1)

            chunk_states(0)
            for hd in range(HG_HEADS):
                n = hd * NCH
                pairs(n)
                for c in range(1, NCH):
                    pairs(n + c)
                    outputs(n + c - 1)
                if hd + 1 < HG_HEADS:
                    chunk_states(hd + 1)
                outputs(n + NCH - 1)
            for hd in range(HG_HEADS):
                pe.wait_ge(S["sq"], hd + 1)
                if hd >= 2:
                    pe.wait_ge(S["log"], hd - 1)
                for lo, hi in ((0, 512), (512, T)):
                    last = nc.tensor.matmul(pP[:, hd % 2, lo:hi], core.ones[:], flat[:, hd * T + lo:hd * T + hi],
                                            start=True, stop=True)
                last.then_inc(S["ms"], 1)


def attention(core, layer, featT, tokV):
    nc = core.nc
    windowed = layer == 0
    HEADS = 8
    dh = 64 if windowed else 128
    scale = float(dh) ** -0.5
    q0, k0 = (F_SQ, F_SK) if windowed else (0, 8)
    rot_tiles = list(range(q0, q0 + (5 if windowed else 10)))
    NBLK = NT if windowed else NTX
    CTX_TILES = [4, 5]
    LATE_FROM = 2

    def key_tiles(b):
        if not windowed:
            return CTX_TILES + list(range(NTX))
        if b >= NTX:
            return CTX_TILES
        return CTX_TILES + [k for k in (b - 1, b, b + 1) if 0 <= k < NTX]

    def runs(keys):
        out = []
        for n, k in enumerate(keys):
            if out and out[-1][1] + out[-1][2] == k and n % 4:
                out[-1][2] += 1
            else:
                out.append([n, k, 1])
        return out

    jobs = [(b, pos) for b in range(NBLK) for pos in range(HEADS)]
    wide = [len(key_tiles(b)) > 4 for b, _ in jobs]
    wide_before = [sum(wide[:n]) for n in range(len(jobs) + 1)]

    def head(pos):
        if windowed:
            kv = pos % 2
            return kv, q0 + pos // 2, k0, slice(HG_W + 64 * kv, HG_W + 64 * kv + 64)
        kv = pos // 4
        return kv, q0 + pos, k0 + kv, slice(P * kv, P * kv + P)

    with ExitStack() as ctx:
        sb, ps, sem = core.opener(ctx, f"att{layer}")
        rot = sb("rot", [P, P])
        cos = sb("cos", [P, NX])
        sin = sb("sin", [P, NX])
        xs = sb("xs", [P, 2, NX])
        xc = sb("xc", [P, 2, NX])
        sq = sb("sq", [P, 2, T])
        inv = None if windowed else sb("inv", [P, len(rot_tiles), T])
        p = sb("p", [P, 2, 768])
        pT = sb("pT", [P, 2, 768])
        otok = sb("otok", [P, HEADS * dh])
        mx = sb("mx", [P, 2])
        negmax = sb("negmax", [P, 16])
        rowsum = sb("rowsum", [P, 2, HEADS])
        esink = sb("esink", [P, 2, HEADS])
        nsink = sb("nsink", [P, HEADS])
        win = sb("win", [P, 2, P], BF16)
        winf = sb("winf", [P, 2, P])
        identb = sb("identb", [P, P], BF16)
        keys2 = sb("keys2", [P, 2, T]) if windowed else None
        pS = ps("pS", [P, 2, 1024])
        pX = ps("pX", [P, 1024])
        pO = ps("pO", [P, HEADS * dh])
        names = ("const", "sq", "ms", "std", "link", "normed", "rot", "cos", "ready", "S", "nb", "exp", "T",
                 "evA", "evB", "PV", "norm", "OT", "OTe", "cast", "es", "ahead", "log")
        S = {n: sem(n) for n in names}
        late = LateModulation(core, sb, ps, sem) if windowed else None
        block = ctx.enter_context(nc.Block())
        consts = core.dram["consts"]

        @block.sync
        def _(sp):
            rc, cc, sc = (C_ROT_SW, C_SW_COS, C_SW_SIN) if windowed else (C_ROT_GA, C_GA_COS, C_GA_SIN)
            sp.dma_start(rot[:], consts[:, rc:rc + P]).then_inc(S["const"], 16)
            sp.dma_start(cos[:], consts[:, cc:cc + NX]).then_inc(S["const"], 16)
            sp.dma_start(sin[:], consts[:, sc:sc + NX]).then_inc(S["const"], 16)
            sp.dma_start(winf[:].rearrange("p a n -> p (a n)"), consts[:, C_WL:C_WL + 2 * P]).then_inc(S["const"], 16)
            if windowed:
                late.load(sp)
                sp.dma_start(core.h[:, 0:NTX, :], core.dram["x"].rearrange("(i p) d -> p i d", p=P)).then_inc(S["ahead"], 16)
                sp.dma_start(core.h[:, NTX:NT, :], core.dram["ctx"].rearrange("(i p) d -> p i d", p=P)).then_inc(S["ahead"], 16)
            for f in range(DC):
                sp.dma_start(out_weights(core, layer, f), core.dram[f"wo{layer}"][f * P:(f + 1) * P, :]).then_inc(S["ahead"], 16)
            if windowed:
                late.store(sp)
            sp.wait_ge(S["ahead"], 16 * (DC + (2 if windowed else 0)))

        @block.gpsimd
        def _(pool):
            pool.wait_ge(S["const"], 64)
            for n, m in enumerate(rot_tiles):
                if not windowed:
                    pool.wait_ge(S["normed"], n + 1)
                if n >= 2:
                    pool.wait_ge(S["ready"], n - 1)
                nc.gpsimd.tensor_tensor(xc[:, n % 2, :], featT[:, m, 0:NX], cos[:], ALU.mult).then_inc(S["cos"], 1)
            if windowed:
                for n in range(len(MOD_LATE)):
                    late.split_pool(pool, n)

        @block.scalar
        def _(act):
            act.wait_ge(S["const"], 64)
            nc.scalar.activation(win[:].rearrange("p a n -> p (a n)"), winf[:].rearrange("p a n -> p (a n)"), ACT.Copy)
            nc.scalar.activation(identb[:], core.ident[:], ACT.Copy).then_inc(S["cast"], 1)
            if not windowed:
                def square(n):
                    w = NX if rot_tiles[n] < k0 else T
                    if n >= 2:
                        act.wait_ge(S["ms"], n - 1)
                    nc.scalar.activation(sq[:, n % 2, 0:w], featT[:, rot_tiles[n], 0:w], ACT.Square).then_inc(S["sq"], 1)

                square(0)
                for n, m in enumerate(rot_tiles):
                    w = NX if m < k0 else T
                    if n + 1 < len(rot_tiles):
                        square(n + 1)
                    act.wait_ge(S["ms"], n + 1)
                    nc.scalar.activation(inv[:, n, 0:w], pS[:, n % 2, 0:w], ACT.Ln, scale=1.0 / dh,
                                         bias=core.eps[:]).then_inc(S["log"], 1)
                for n, m in enumerate(rot_tiles):
                    w = NX if m < k0 else T
                    act.wait_ge(S["log"], n + 1)
                    nc.scalar.activation(inv[:, n, 0:w], inv[:, n, 0:w], ACT.Exp, scale=-0.5).then_inc(S["std"], 1)

            def exps(n):
                b, pos = jobs[n]
                w = len(key_tiles(b)) * P
                act.wait_ge(S["nb"], n + 1)
                if n >= 2:
                    act.wait_ge(S["T"], n - 1)
                if b >= 2:
                    act.wait_ge(S["norm"], b - 1)
                nb = negmax[:, n % 16:n % 16 + 1]
                nc.scalar.activation(p[:, n % 2, 0:w], pS[:, n % 2, 0:w], ACT.Exp, scale=scale, bias=nb,
                                     accum_out=rowsum[:, b % 2, pos:pos + 1]).then_inc(S["exp"], 1)
                if windowed:
                    nc.scalar.activation(esink[:, b % 2, pos:pos + 1], core.vecs[:, V_SINK + pos:V_SINK + pos + 1],
                                         ACT.Exp, bias=nb).then_inc(S["es"], 1)

            def move_weights(n):
                w = min(len(key_tiles(jobs[n][0])), 4) * P
                act.wait_ge(S["T"], n + 1)
                if n >= 2:
                    act.wait_ge(S["PV"], n - 1)
                nc.scalar.activation(pT[:, n % 2, 0:w], pX[:, 0:w], ACT.Copy).then_inc(S["evA"], 1)

            def move_block(b):
                act.wait_ge(S["OT"], b + 1)
                n = HEADS * dh // P
                nc.scalar.activation(featT[:, q0:q0 + n, b * P:(b + 1) * P],
                                     pX[:, 0:n * P].rearrange("p (m t) -> p m t", t=P), ACT.Copy).then_inc(S["OTe"], 1)

            exps(0)
            for n, (b, pos) in enumerate(jobs):
                if n + 1 < len(jobs):
                    exps(n + 1)
                move_weights(n)
                if pos == 0 and b > 0:
                    move_block(b - 1)
            move_block(NBLK - 1)

        @block.vector
        def _(dve):
            link = linker(dve, S["link"])
            link(nc.vector.tensor_scalar(nsink[:], core.vecs[:, V_SINK:V_SINK + HEADS], -1.0, None, ALU.mult))
            dve.wait_ge(S["const"], 64)

            def normalise(n):
                m = rot_tiles[n]
                w = NX if m < k0 else T
                x = featT[:, m, 0:w]
                gain = V_GAQ if m < k0 else V_GAK
                dve.wait_ge(S["std"], n + 1)
                nc.vector.scalar_tensor_tensor(out=x, in0=x, scalar=core.vecs[:, gain:gain + 1],
                                               in1=inv[:, n, 0:w], op0=ALU.mult,
                                               op1=ALU.mult).then_inc(S["normed"], 1)

            def rotate(n):
                m = rot_tiles[n]
                dve.wait_ge(S["rot"], n + 1)
                link(nc.vector.tensor_tensor(xs[:, n % 2, :], pX[:, 512 * (n % 2):512 * (n % 2) + 512], sin[:], ALU.mult))
                dve.wait_ge(S["cos"], n + 1)
                nc.vector.tensor_tensor(featT[:, m, 0:NX], xs[:, n % 2, :], xc[:, n % 2, :],
                                        ALU.add).then_inc(S["ready"], 1)

            for n in range(len(rot_tiles)):
                if not windowed:
                    normalise(n)
                if n >= 1:
                    rotate(n - 1)
            rotate(len(rot_tiles) - 1)
            if windowed:
                dve.wait_ge(S["ready"], len(rot_tiles))
                link(nc.vector.memset(keys2[:], 0.0))
                nc.vector.tensor_copy(keys2[0:64, 0, :], featT[0:64, k0, :])
                nc.vector.tensor_copy(keys2[64:128, 1, :], featT[64:128, k0, :]).then_inc(S["ready"], 1)

            def maxima(n):
                b, pos = jobs[n]
                w = len(key_tiles(b)) * P
                dve.wait_ge(S["S"], n + 1)
                link(nc.vector.tensor_reduce(mx[:, n % 2:n % 2 + 1], pS[:, n % 2, 0:w], AX, ALU.max))
                if windowed:
                    ins = nc.vector.tensor_scalar(negmax[:, n % 16:n % 16 + 1], mx[:, n % 2:n % 2 + 1], -scale,
                                                  nsink[:, pos:pos + 1], ALU.mult, ALU.min)
                else:
                    ins = nc.vector.tensor_scalar(negmax[:, n % 16:n % 16 + 1], mx[:, n % 2:n % 2 + 1], -scale,
                                                  None, ALU.mult)
                ins.then_inc(S["nb"], 1)

            def move_rest(n):
                if wide[n]:
                    w = len(key_tiles(jobs[n][0])) * P
                    dve.wait_ge(S["T"], n + 1)
                    if n >= 2:
                        dve.wait_ge(S["PV"], n - 1)
                    nc.vector.tensor_copy(pT[:, n % 2, 512:w], pX[:, 512:w]).then_inc(S["evB"], 1)

            def divide(b):
                dve.wait_ge(S["PV"], (b + 1) * HEADS)
                rs = rowsum[:, b % 2, :]
                if windowed:
                    dve.wait_ge(S["es"], (b + 1) * HEADS)
                    link(nc.vector.tensor_tensor(rs, rs, esink[:, b % 2, :], ALU.add))
                link(nc.vector.reciprocal(rs, rs))
                if b > 0:
                    dve.wait_ge(S["OT"], b)
                nc.vector.tensor_tensor(otok[:].rearrange("p (h d) -> p h d", d=dh),
                                        pO[:].rearrange("p (h d) -> p h d", d=dh),
                                        rs.unsqueeze(2).to_broadcast([P, HEADS, dh]), ALU.mult).then_inc(S["norm"], 1)

            maxima(0)
            for n, (b, pos) in enumerate(jobs):
                if n + 1 < len(jobs):
                    maxima(n + 1)
                move_rest(n)
                if pos == 0 and b > 0:
                    divide(b - 1)
                g = n - LATE_FROM - 1
                if windowed and 0 <= g < len(MOD_LATE):
                    late.copy_line(dve, g)
                if windowed and 0 <= g + 2 < len(MOD_LATE):
                    late.split(dve, g + 2)
                if windowed and n == LATE_FROM + len(MOD_LATE) + 1:
                    late.finish(dve, link)
            divide(NBLK - 1)
            if windowed:
                late.move_rows(dve)

        @block.tensor
        def _(pe):
            pe.wait_ge(S["const"], 64)

            def mean_squares(n):
                w = NX if rot_tiles[n] < k0 else T
                pe.wait_ge(S["sq"], n + 1)
                if n >= 2:
                    pe.wait_ge(S["log"], n - 1)
                for lo in range(0, w, 512):
                    hi = min(lo + 512, w)
                    last = nc.tensor.matmul(pS[:, n % 2, lo:hi], core.ones[:], sq[:, n % 2, lo:hi],
                                            start=True, stop=True)
                last.then_inc(S["ms"], 1)

            if not windowed:
                for n in range(len(rot_tiles)):
                    mean_squares(n)
            for n, m in enumerate(rot_tiles):
                if not windowed:
                    pe.wait_ge(S["normed"], n + 1)
                if n >= 2:
                    pe.wait_ge(S["ready"], n - 1)
                nc.tensor.matmul(pX[:, 512 * (n % 2):512 * (n % 2) + 512], rot[:], featT[:, m, 0:NX],
                                 start=True, stop=True).then_inc(S["rot"], 1)
            pe.wait_ge(S["ready"], len(rot_tiles) + (1 if windowed else 0))
            pe.wait_ge(S["cast"], 1)

            def scores(n):
                b, pos = jobs[n]
                kv, qt, kt, _ = head(pos)
                keys = key_tiles(b)
                if n >= 2:
                    pe.wait_ge(S["exp"], n - 1)
                for at, k, w in runs(keys):
                    masked = [(j, 0 if keys[j] == b - 1 else 1) for j in range(at, at + w)
                              if windowed and b < NTX and k < NTX and keys[j] != b]
                    last = nc.tensor.matmul(pS[:, n % 2, at * P:(at + w) * P], featT[:, qt, b * P:(b + 1) * P],
                                            (keys2[:, kv, k * P:(k + w) * P] if windowed else
                                             featT[:, kt, k * P:(k + w) * P]), start=True, stop=not masked)
                    for x, (j, side) in enumerate(masked):
                        last = nc.tensor.matmul(pS[:, n % 2, j * P:(j + 1) * P], identb[:], win[:, side, :],
                                                start=False, stop=(x == len(masked) - 1))
                last.then_inc(S["S"], 1)

            def turn_weights(n):
                b, _ = jobs[n]
                pe.wait_ge(S["exp"], n + 1)
                if n >= 1:
                    pe.wait_ge(S["evA"], n)
                    if wide_before[n]:
                        pe.wait_ge(S["evB"], wide_before[n])
                if b > 1 or (b == 1 and jobs[n][1] > 0):
                    pe.wait_ge(S["OTe"], b if jobs[n][1] > 0 else b - 1)
                for j in range(len(key_tiles(b))):
                    last = nc.tensor.transpose(pX[:, j * P:(j + 1) * P], p[:, n % 2, j * P:(j + 1) * P], core.ident[:])
                last.then_inc(S["T"], 1)

            def values(n):
                b, pos = jobs[n]
                _, _, _, cols = head(pos)
                pe.wait_ge(S["evA"], n + 1)
                if wide[n]:
                    pe.wait_ge(S["evB"], wide_before[n + 1])
                if b > 0 and pos == 0:
                    pe.wait_ge(S["norm"], b)
                keys = key_tiles(b)
                for j, k in enumerate(keys):
                    last = nc.tensor.matmul(pO[:, pos * dh:(pos + 1) * dh], pT[:, n % 2, j * P:(j + 1) * P],
                                            tokV[:, k, cols], start=(j == 0), stop=(j == len(keys) - 1))
                last.then_inc(S["PV"], 1)

            def turn_block(b, n):
                pe.wait_ge(S["norm"], b + 1)
                pe.wait_ge(S["evA"], n)
                if wide_before[n]:
                    pe.wait_ge(S["evB"], wide_before[n])
                for j in range(HEADS * dh // P):
                    last = nc.tensor.transpose(pX[:, j * P:(j + 1) * P], otok[:, j * P:(j + 1) * P], core.ident[:])
                last.then_inc(S["OT"], 1)

            scores(0)
            scores(1)
            for n, (b, pos) in enumerate(jobs):
                turn_weights(n)
                if n + 2 < len(jobs):
                    scores(n + 2)
                values(n)
                if pos == 0 and b > 0:
                    turn_block(b - 1, n + 1)
                if windowed and 0 <= n - LATE_FROM < len(MOD_LATE):
                    late.multiply(pe, n - LATE_FROM)
                if windowed and 0 <= n - LATE_FROM - 1 < len(MOD_LATE):
                    late.turn(pe, n - LATE_FROM - 1)
                if windowed and n == LATE_FROM + len(MOD_LATE) + 1:
                    late.turn_rows(pe)
            turn_block(NBLK - 1, len(jobs))


def features(core, count):
    return core.ring[:, 0:count * T].rearrange("p (m t) -> p m t", t=T)


def out_weights(core, layer, f):
    if layer == 0:
        at = F_FB * T + f * D if f < 6 else F_Q * T + (f - 6) * D
    else:
        at = FEAT1 * T + f * D
    return core.ring[:, at:at + D]


def mix_gate(core, layer, kind):
    if layer == 0:
        at = (F_Q * T + 2 * D, F_SK * T)[kind]
    else:
        at = 8 * T
    return core.ring[:, at:at + D]


def peer(core, layer):
    nc = core.nc
    tiles = NT if layer == 0 else NTX
    GROUP = 2
    DIAGS = 4
    EARLY = 4
    mixed = [F_FF, F_FF + 1, F_FF + 2, F_FF + 3, F_SQ, F_SQ + 1, F_SQ + 2, F_SQ + 3] if layer == 0 else list(range(8))
    kinds = 2 if layer == 0 else 1
    MOVE_Q = (30, 38, 46, 54)
    KEY_SCORES = (36, 44, 52, 58)
    MOVE_SCORES = (44, 52, 60, 64)
    MIXED_FIRST = 2 if layer == 0 else 1
    DECODE = (89, 90, 92, 93, 95, 97, 98)
    with ExitStack() as ctx:
        sb, ps, sem = core.opener(ctx, f"peer{layer}")
        h = core.h
        wq = sb("wq", [P, DC, 2 * PH * P])
        skT = sb("skT", [P, 2 * PH, KEYS])
        ring = core.ring[:].rearrange("p (r d) -> p r d", r=RING)
        f_cur = sb("f_cur", [P, D])
        f_next = sb("f_next", [P, D])
        rows = sb("rows", [P, 2, D])
        fT = rows[:, 0, :].rearrange("p (c t) -> p c t", t=P)
        gate = sb("gate", [P, D])
        gate_row = gate[:]
        shift_row, gain_row = rows[:, 0, :], rows[:, 1, :]
        qT = sb("qT", [P, 2, 4, P])
        sc = sb("sc", [P, 2 * PH, KEYS])
        diag = sb("diag", [P, DIAGS, GROUP, P])
        top = sb("top", [P, 2 * PH, TOPK])
        topi = sb("topi", [P, 2 * PH, TOPK], U32)
        topf = sb("topf", [P, 2 * PH, TOPK])
        best = sb("best", [P, PH, TOPK])
        besti = sb("besti", [P, PICKS], U32)
        low = sb("low", [P, PICKS], U32)
        lowf = sb("lowf", [P, PICKS])
        highf = sb("highf", [P, PICKS])
        pick1 = sb("pick1", [P, PICKS])
        idx_next = sb("idx_next", [P, PICKS], U32)
        idx_cur = sb("idx_cur", [P, PICKS], U32)
        gate_next = sb("gate_next", [P, PH, TOPK])
        gate_cur = sb("gate_cur", [P, PICKS])
        gsum = sb("gsum", [P, PH])
        dots = sb("dots", [P, PICKS])
        acts = sb("acts", [P, PICKS])
        std = sb("std", [P, 2])
        iota = sb("iota", [P, 32])
        acc = ps("acc", [P, D])
        acc2 = ps("acc2", [P, D])
        stage = ps("stage", [P, 4, 512])
        names = ("w", "iota", "rows", "gate", "ssq", "std", "fn", "tr", "fT", "q", "qT", "s", "sc", "rt", "gsub", "gexp",
                 "routed", "idxA", "idxB", "free", "dot", "gelu", "diag", "accfree", "cur", "h",
                 "passed_pool", "passed_dve", "mixgate", "mixed", "gated", "added", "group")
        S = {n: sem(n) for n in names}
        landed = [sem(f"landed{i}") for i in range(RING)]
        block = ctx.enter_context(nc.Block())
        modr = core.dram["modr"]
        NEG = -3.0e38

        @block.sync
        def _(sp):
            sp.dma_start(iota[:], core.dram["consts"][:, C_IOTA:C_IOTA + 32]).then_inc(S["iota"], 16)

            def modulation_rows(tile):
                kind = 0 if tile < NTX else 1
                if tile > 0:
                    sp.wait_ge(S["q"], 4 * tile)
                src = modr[layer, kind, 3 * D:4 * D]
                sp.dma_start(shift_row, src.partition_broadcast(P)).then_inc(S["rows"], 16)
                if tile in (0, NTX):
                    if tile > 0:
                        sp.wait_ge(S["fn"], tile)
                    src = modr[layer, kind, 4 * D:5 * D]
                    sp.dma_start(gain_row, src.partition_broadcast(P)).then_inc(S["rows"], 16)
                else:
                    sp.sem_inc(S["rows"], 16)

            def gate_rows(tile):
                kind = 0 if tile < NTX else 1
                if tile in (0, NTX):
                    if tile > 0:
                        sp.wait_ge(S["accfree"], tile + 1)
                    src = modr[layer, kind, 5 * D:6 * D]
                    sp.dma_start(gate_row, src.partition_broadcast(P)).then_inc(S["gate"], 16)
                else:
                    sp.wait_ge(S["gate"], 16 * tile)
                    sp.sem_inc(S["gate"], 16)

            for kind in range(kinds):
                sp.dma_start(mix_gate(core, layer, kind), modr[layer, kind, 2 * D:3 * D].partition_broadcast(P)).then_inc(
                    S["mixgate"], 16)
            modulation_rows(0)
            sp.dma_start(skT[:], core.dram[f"skT{layer}"].rearrange("m d n -> d m n")).then_inc(S["w"], 16)
            src = core.dram[f"wq{layer}"].rearrange("(c p) n -> p c n", p=P)
            for c in range(DC):
                sp.dma_start(wq[:, c, :], src[:, c, :]).then_inc(S["w"], 16)
            for tile in range(tiles):
                if tile + 1 < tiles:
                    modulation_rows(tile + 1)
                gate_rows(tile)

        @block.gpsimd
        def _(pool):
            def copy_half(tile, half):
                lo = 64 * half
                wait_plain(pool, S["routed"], tile + 1, S["passed_pool"])
                nc.gpsimd.tensor_copy(idx_cur[:, lo:lo + 64], idx_next[:, lo:lo + 64]).then_inc(
                    S["idxB" if half else "idxA"], 1)

            def gathers(tile, last):
                for k in range(PICKS):
                    if k == 0:
                        wait_plain(pool, S["idxA"], tile + 1, S["passed_pool"])
                    if k == 16:
                        copy_half(tile, 1)
                    if k == 64:
                        wait_plain(pool, S["idxB"], tile + 1, S["passed_pool"])
                    if k == 112 and not last:
                        copy_half(tile + 1, 0)
                    wait_plain(pool, S["free"], tile * PICKS + (k + 1), S["passed_pool"])
                    nc.gpsimd.indirect_dma_start(
                        ring[:, k % RING, :], None, core.dram[f"uv{layer}"],
                        bass.IndirectOffsetOnAxis(ap=idx_cur[:, k:k + 1], axis=0)).then_inc(landed[k % RING], 16)

            copy_half(0, 0)
            with pool.Fori(0, tiles - 1) as tile:
                gathers(tile, False)
            gathers(tiles - 1, True)

        @block.scalar
        def _(act):
            def root(tile):
                act.wait_ge(S["ssq"], tile + 1)
                nc.scalar.activation(std[:, 1:2], std[:, 0:1], ACT.Sqrt, scale=1.0 / D,
                                     bias=core.eps[:]).then_inc(S["std"], 1)

            def move_f(tile):
                act.wait_ge(S["tr"], tile + 1)
                nc.scalar.activation(rows[:, 0, :], stage[:, 0:2].rearrange("p a n -> p (a n)"),
                                     ACT.Copy).then_inc(S["fT"], 1)

            def move_q(tile, j):
                act.wait_ge(S["q"], tile * 4 + (j + 1))
                if j >= 2:
                    act.wait_ge(S["s"], tile * 4 + (j - 1))
                nc.scalar.activation(qT[:, j % 2].rearrange("p m t -> p (m t)"), stage[:, 2 + j % 2, :],
                                     ACT.Copy).then_inc(S["qT"], 1)

            def move_scores(tile, j):
                act.wait_ge(S["s"], tile * 4 + (j + 1))
                nc.scalar.activation(sc[:, 4 * j:4 * j + 4, :].rearrange("p m t -> p (m t)"), stage[:, j % 2, :],
                                     ACT.Copy).then_inc(S["sc"], 1)

            def gate_exp(tile):
                act.wait_ge(S["gsub"], tile + 1)
                nc.scalar.activation(gate_next[:], gate_next[:], ACT.Exp).then_inc(S["gexp"], 1)

            def experts(tile, route):
                for k in range(PICKS):
                    if route:
                        if k == 6:
                            root(tile + 1)
                        if k == 20:
                            move_f(tile + 1)
                        if k in MOVE_Q:
                            move_q(tile + 1, MOVE_Q.index(k))
                        if k in MOVE_SCORES:
                            move_scores(tile + 1, MOVE_SCORES.index(k))
                        if k == 94:
                            gate_exp(tile + 1)
                    if k % GROUP == GROUP - 1:
                        g = k - GROUP + 1
                        act.wait_ge(S["dot"], tile * PICKS + (k + 1))
                        nc.scalar.activation(acts[:, g:k + 1], dots[:, g:k + 1], ACT.Gelu).then_inc(S["gelu"], 1)

            root(0)
            move_f(0)
            for j in range(5):
                if j < 4:
                    move_q(0, j)
                if j > 0:
                    move_scores(0, j - 1)
            gate_exp(0)
            with act.Fori(0, tiles - 1) as tile:
                experts(tile, True)
            experts(tiles - 1, False)

        @block.vector
        def _(dve):
            STEPS = 24

            def linker_of(tile):
                count = [0]

                def link(ins):
                    count[0] += 1
                    ins.then_inc(S["rt"], 1)
                    wait_plain(dve, S["rt"], tile * STEPS + count[0], S["passed_dve"])

                return link, count

            def dyn(x, tile):
                return x[:, tile, :] if isinstance(tile, int) else x[:, bass.ds(tile, 1), :].rearrange("p a d -> p (a d)")

            def squares(tile, link):
                if not isinstance(tile, int):
                    dve.wait_ge(S["tr"], tile)
                    dve.wait_ge(S["h"], tile)
                nc.vector.scalar_tensor_tensor(out=f_next[:], in0=dyn(h, tile), scalar=1.0, in1=dyn(h, tile),
                                               op0=ALU.mult, op1=ALU.mult, accum_out=std[:, 0:1]).then_inc(S["ssq"], 1)

            def normalise(tile, link):
                wait_plain(dve, S["std"], tile + 1, S["passed_dve"])
                link(nc.vector.reciprocal(std[:, 1:2], std[:, 1:2]))
                dve.wait_ge(S["rows"], tile * 32 + 32)
                link(nc.vector.scalar_tensor_tensor(out=f_next[:], in0=dyn(h, tile), scalar=std[:, 1:2],
                                                    in1=gain_row, op0=ALU.mult, op1=ALU.mult))
                nc.vector.tensor_tensor(f_next[:], f_next[:], shift_row, ALU.add).then_inc(S["fn"], 1)

            def best8(dst, src, count):
                for m in range(count):
                    last = nc.vector.max(dst(m), src(m))
                return last

            def scores_of(m):
                return sc[:, m, :]

            def search_keys(tile, link, step):
                if step == 0:
                    wait_plain(dve, S["sc"], tile * 4 + 4, S["passed_dve"])
                    link(best8(lambda m: top[:, m, 0:8], scores_of, 2 * PH))
                if step == 1:
                    for m in range(2 * PH):
                        last = nc.vector.max_index(topi[:, m, 0:8], top[:, m, 0:8], sc[:, m, :])
                    link(last)
                if step == 2:
                    for m in range(2 * PH):
                        last = nc.vector.match_replace(sc[:, m, :], top[:, m, 0:8], sc[:, m, :], NEG)
                    link(last)
                if step == 3:
                    link(best8(lambda m: top[:, m, 8:16], scores_of, 2 * PH))
                if step == 4:
                    for m in range(2 * PH):
                        last = nc.vector.max_index(topi[:, m, 8:16], top[:, m, 8:16], sc[:, m, :])
                    link(last)
                    nc.vector.tensor_copy(topf[:], topi[:])

            def search_group(j, link):
                heads = range(4 * j, 4 * j + 4)
                dve.wait_ge(S["sc"], j + 1)
                for half in range(2):
                    found = slice(8 * half, 8 * half + 8)
                    for m in heads:
                        last = nc.vector.max(top[:, m, found], sc[:, m, :])
                    link(last)
                    for m in heads:
                        last = nc.vector.max_index(topi[:, m, found], top[:, m, found], sc[:, m, :])
                    link(last)
                    if half == 0:
                        for m in heads:
                            last = nc.vector.match_replace(sc[:, m, :], top[:, m, found], sc[:, m, :], NEG)
                        link(last)

            cand = sc[:].rearrange("p m n -> p (m n)").rearrange("p (h n) -> p h n", n=TOPK * TOPK)
            by_head = top[:].rearrange("p (h s) k -> p h s k", s=2)
            fkeys = topf[:].rearrange("p (h s) k -> p h s k", s=2)

            def search_candidates(tile, link, step):
                if step == 0:
                    link(nc.vector.tensor_tensor(
                        cand.rearrange("p h (a b) -> p h a b", b=TOPK),
                        by_head[:, :, 0, :].unsqueeze(3).to_broadcast([P, PH, TOPK, TOPK]),
                        by_head[:, :, 1, :].unsqueeze(2).to_broadcast([P, PH, TOPK, TOPK]), ALU.add))
                if step == 1:
                    link(best8(lambda m: best[:, m, 0:8], lambda m: cand[:, m, :], PH))
                if step == 2:
                    for m in range(PH):
                        last = nc.vector.max_index(besti[:, m * TOPK:m * TOPK + 8], best[:, m, 0:8], cand[:, m, :])
                    link(last)
                if step == 3:
                    for m in range(PH):
                        last = nc.vector.match_replace(cand[:, m, :], best[:, m, 0:8], cand[:, m, :], NEG)
                    link(last)
                if step == 4:
                    link(best8(lambda m: best[:, m, 8:16], lambda m: cand[:, m, :], PH))
                if step == 5:
                    for m in range(PH):
                        last = nc.vector.max_index(besti[:, m * TOPK + 8:m * TOPK + 16], best[:, m, 8:16],
                                                   cand[:, m, :])
                    link(last)

            def softmax_in(tile):
                nc.vector.tensor_tensor(gate_next[:], best[:], best[:, :, 0:1].to_broadcast([P, PH, TOPK]),
                                        ALU.subtract).then_inc(S["gsub"], 1)

            def decode(tile, link, step):
                onehot = sc[:].rearrange("p m n -> p (m n)").rearrange("p (k j) -> p k j", j=TOPK)
                byh = onehot.rearrange("p (h k) j -> p h k j", k=TOPK)
                if step == 0:
                    nc.vector.tensor_scalar(low[:], besti[:], TOPK - 1, None, ALU.bitwise_and)
                    link(nc.vector.tensor_copy(highf[:], besti[:]))
                    link(nc.vector.tensor_copy(lowf[:], low[:]))
                    link(nc.vector.tensor_tensor(highf[:], highf[:], lowf[:], ALU.subtract))
                if step > 0:
                    side, part = divmod(step - 1, 3)
                    which = (highf, lowf)[side]
                    code = iota[:, 16 * side:16 * side + 16]
                if step > 0 and part == 0:
                    link(nc.vector.tensor_tensor(onehot, which[:].unsqueeze(2).to_broadcast([P, PICKS, TOPK]),
                                                 code.unsqueeze(1).to_broadcast([P, PICKS, TOPK]), ALU.is_equal))
                if step > 0 and part == 1:
                    link(nc.vector.tensor_tensor(byh, byh, fkeys[:, :, side, :].unsqueeze(2).to_broadcast(
                        [P, PH, TOPK, TOPK]), ALU.mult))
                if step > 0 and part == 2:
                    link(nc.vector.tensor_reduce((pick1, lowf)[side][:], onehot, AX, ALU.add))

            def finish_routing(tile, link, count):
                wait_plain(dve, S["gexp"], tile + 1, S["passed_dve"])
                if not isinstance(tile, int):
                    wait_plain(dve, S["idxB"], tile, S["passed_dve"])
                link(nc.vector.tensor_reduce(gsum[:], gate_next[:], AX, ALU.add))
                nc.vector.reciprocal(gsum[:], gsum[:]).then_inc(S["rt"], 1)
                count[0] += 1
                dve.wait_ge(S["rt"], tile * STEPS + count[0])
                nc.vector.tensor_tensor(gate_next[:], gate_next[:],
                                        gsum[:].unsqueeze(2).to_broadcast([P, PH, TOPK]), ALU.mult)
                nc.vector.scalar_tensor_tensor(out=idx_next[:], in0=pick1[:], scalar=float(KEYS), in1=lowf[:],
                                               op0=ALU.mult, op1=ALU.add).then_inc(S["routed"], 1)

            def take_over(tile):
                wait_plain(dve, S["routed"], tile + 1, S["passed_dve"])
                if not isinstance(tile, int):
                    dve.wait_ge(S["dot"], tile * PICKS)
                    dve.wait_ge(S["diag"], tile * (PICKS // GROUP))
                nc.vector.tensor_copy(f_cur[:], f_next[:])
                nc.vector.tensor_copy(gate_cur[:], gate_next[:].rearrange("p h k -> p (h k)")).then_inc(S["cur"], 1)

            def diagonals(tile, g):
                n = tile * (PICKS // GROUP) + (g + 1)
                dve.wait_ge(S["gelu"], n)
                dve.wait_ge(S["free"], tile * PICKS + (g * GROUP + RING - (DIAGS - 1) * GROUP))
                for j in range(GROUP):
                    k = g * GROUP + j
                    last = nc.vector.tensor_scalar(diag[:, g % DIAGS, j, :], core.ident[:], acts[:, k:k + 1],
                                                   gate_cur[:, k:k + 1], ALU.mult, ALU.mult)
                last.then_inc(S["diag"], 1)

            def end_tile(tile):
                dve.wait_ge(S["free"], tile * PICKS + (PICKS + RING))
                dve.wait_ge(S["gate"], tile * 16 + 16)
                nc.vector.tensor_tensor(f_next[:], acc[:], gate_row, ALU.mult).then_inc(S["accfree"], 1)
                dve.wait_ge(S["accfree"], tile + 2)
                nc.vector.tensor_tensor(dyn(h, tile), dyn(h, tile), f_next[:], ALU.add).then_inc(S["h"], 1)

            def dot(tile, k):
                dve.wait_ge(landed[k % RING], tile * (PICKS // RING * 16) + 16 * (k // RING + 1))
                slot = ring[:, k % RING, 0:D]
                nc.vector.tensor_tensor_reduce(slot, slot, f_cur[:], 1.0, 0.0, ALU.mult, ALU.add,
                                               dots[:, k:k + 1]).then_inc(S["dot"], 1)

            def dot_and_diagonals(tile, k):
                dot(tile, k)
                if k % GROUP == 0 and k > 0:
                    diagonals(tile, k // GROUP - 1)

            def first_dots(tile):
                dve.wait_ge(S["cur"], tile + 1)
                for k in range(EARLY):
                    dot_and_diagonals(tile, k)

            def experts(tile, route):
                if route:
                    link, count = linker_of(tile + 1)
                for k in range(EARLY, PICKS):
                    if route:
                        nxt = tile + 1
                        if k == 4:
                            squares(nxt, link)
                        if k == 10:
                            normalise(nxt, link)
                        if 66 <= k < 76 and k % 2 == 0:
                            search_keys(nxt, link, (k - 66) // 2)
                        if 76 <= k < 88 and k % 2 == 0:
                            search_candidates(nxt, link, (k - 76) // 2)
                        if k == 88:
                            softmax_in(nxt)
                        if k in DECODE:
                            decode(nxt, link, DECODE.index(k))
                        if k == 102:
                            finish_routing(nxt, link, count)
                            assert count[0] == STEPS, count
                    dot_and_diagonals(tile, k)
                diagonals(tile, PICKS // GROUP - 1)
                if route:
                    take_over(tile + 1)
                    first_dots(tile + 1)
                end_tile(tile)

            gated = diag[:].rearrange("p a g n -> p (a g n)")

            def add_mixed(i):
                dve.wait_ge(S["mixed"], i + 1)
                if i > 0:
                    dve.wait_ge(S["added"], i)
                nc.vector.tensor_tensor(gated, (acc, acc2)[i % 2][:], mix_gate(core, layer, 0 if i < NTX else 1),
                                        ALU.mult).then_inc(S["gated"], 1)
                dve.wait_ge(S["gated"], i + 1)
                nc.vector.tensor_tensor(h[:, i, :], h[:, i, :], gated, ALU.add).then_inc(S["added"], 1)

            dve.wait_ge(S["iota"], 16)
            dve.wait_ge(S["mixgate"], 16 * kinds)
            link, count = linker_of(0)
            add_mixed(0)
            dve.wait_ge(S["added"], 1)
            squares(0, link)
            normalise(0, link)
            for i in range(1, MIXED_FIRST):
                add_mixed(i)
            left = list(range(MIXED_FIRST, tiles))
            link_group = linker(dve, S["group"])
            for j in range(4):
                search_group(j, link_group)
            nc.vector.tensor_copy(topf[:], topi[:])
            dve.sem_inc(S["rt"], 5)
            count[0] += 5
            for step in range(6):
                search_candidates(0, link, step)
                if step in (2, 4):
                    add_mixed(left.pop(0))
            softmax_in(0)
            for step in range(len(DECODE)):
                decode(0, link, step)
            finish_routing(0, link, count)
            for i in left:
                add_mixed(i)
            dve.wait_ge(S["added"], tiles)
            dve.sem_inc(S["accfree"], 1)
            dve.sem_inc(S["free"], RING)
            dve.sem_inc(S["h"], 1)
            take_over(0)
            first_dots(0)
            with dve.Fori(0, tiles - 1) as tile:
                experts(tile, True)
            experts(tiles - 1, False)

        @block.tensor
        def _(pe):
            def turn_f(tile):
                pe.wait_ge(S["fn"], tile + 1)
                for c in range(DC):
                    last = nc.tensor.transpose(stage[:, c // 4, (c % 4) * P:(c % 4 + 1) * P],
                                               f_next[:, c * P:(c + 1) * P], core.ident[:])
                last.then_inc(S["tr"], 1)

            def queries(tile, m):
                if m == 0:
                    pe.wait_ge(S["fT"], tile + 1)
                if m % 4 == 0 and m >= 8:
                    pe.wait_ge(S["qT"], tile * 4 + (m // 4 - 1))
                for c in range(DC):
                    last = nc.tensor.matmul(stage[:, 2 + (m // 4) % 2, (m % 4) * P:(m % 4 + 1) * P],
                                            wq[:, c, m * P:(m + 1) * P], fT[:, c, :], start=(c == 0), stop=(c == DC - 1))
                if m % 4 == 3:
                    last.then_inc(S["q"], 1)

            def key_scores(tile, j):
                pe.wait_ge(S["qT"], tile * 4 + (j + 1))
                if j >= 2:
                    pe.wait_ge(S["sc"], tile * 4 + (j - 1))
                for m in range(4 * j, 4 * j + 4):
                    last = nc.tensor.matmul(stage[:, j % 2, (m % 4) * P:(m % 4 + 1) * P], qT[:, j % 2, m % 4, :], skT[:, m, :],
                                            start=True, stop=True)
                last.then_inc(S["s"], 1)

            def experts(tile, route):
                pe.wait_ge(S["accfree"], tile + 1)
                for k in range(PICKS):
                    if route:
                        if k == 14:
                            turn_f(tile + 1)
                        if 18 <= k < 50 and k % 2 == 0:
                            queries(tile + 1, (k - 18) // 2)
                        if k in KEY_SCORES:
                            key_scores(tile + 1, KEY_SCORES.index(k))
                    if k % GROUP == 0:
                        pe.wait_ge(S["diag"], tile * (PICKS // GROUP) + (k // GROUP + 1))
                    for half in range(2):
                        last = nc.tensor.matmul(acc[:, half * 512:half * 512 + 512], diag[:, (k // GROUP) % DIAGS, k % GROUP, :],
                                                ring[:, k % RING, D + half * 512:D + half * 512 + 512],
                                                start=(k == 0), stop=(k == PICKS - 1))
                    last.then_inc(S["free"], 1)

            def mixed_out(i):
                if i >= 2:
                    pe.wait_ge(S["gated"], i - 1)
                for half in range(2):
                    for f, m in enumerate(mixed):
                        last = nc.tensor.matmul((acc, acc2)[i % 2][:, half * 512:half * 512 + 512],
                                                core.ring[:, m * T + i * P:m * T + (i + 1) * P],
                                                out_weights(core, layer, f)[:, half * 512:half * 512 + 512],
                                                start=(f == 0), stop=(f == DC - 1))
                last.then_inc(S["mixed"], 1)

            for i in range(MIXED_FIRST):
                mixed_out(i)
            turn_f(0)
            pe.wait_ge(S["w"], 16 * (1 + DC))
            for j in range(5):
                if j < 4:
                    for m in range(4 * j, 4 * j + 4):
                        queries(0, m)
                if j > 0:
                    key_scores(0, j - 1)
            for i in range(MIXED_FIRST, tiles):
                mixed_out(i)
            with pe.Fori(0, tiles - 1) as tile:
                experts(tile, True)
            experts(tiles - 1, False)


def final_norm(core):
    nc = core.nc
    with ExitStack() as ctx:
        sb, ps, sem = core.opener(ctx, "fin")
        gain = sb("gain", [P, D])
        out = sb("out", [P, NTX, D])
        ssq = sb("ssq", [P, NTX])
        s_gain, s_ssq, s_std, s_link, s_y, s_out = (sem(n) for n in ("gain", "ssq", "std", "link", "y", "out"))
        block = ctx.enter_context(nc.Block())

        @block.sync
        def _(sp):
            sp.dma_start(gain[:], core.dram["final_g"].partition_broadcast(P)).then_inc(s_gain, 16)
            dst = core.dram["out"].rearrange("(i p) d -> p i d", p=P)
            for i in range(NTX):
                sp.wait_ge(s_y, i + 1)
                sp.dma_start(dst[:, i, :], out[:, i, :]).then_inc(s_out, 16)
            sp.wait_ge(s_out, 16 * NTX)

        @block.scalar
        def _(act):
            for i in range(NTX):
                nc.scalar.activation(out[:, i, :], core.h[:, i, :], ACT.Square,
                                     accum_out=ssq[:, i:i + 1]).then_inc(s_ssq, 1)
            act.wait_ge(s_ssq, NTX)
            nc.scalar.activation(ssq[:], ssq[:], ACT.Sqrt, scale=1.0 / D, bias=core.eps[:]).then_inc(s_std, 1)

        @block.vector
        def _(dve):
            link = linker(dve, s_link)
            dve.wait_ge(s_std, 1)
            link(nc.vector.reciprocal(ssq[:], ssq[:]))
            dve.wait_ge(s_gain, 16)
            for i in range(NTX):
                nc.vector.scalar_tensor_tensor(out=out[:, i, :], in0=core.h[:, i, :], scalar=ssq[:, i:i + 1],
                                               in1=gain[:], op0=ALU.mult, op1=ALU.mult).then_inc(s_y, 1)


PHASES = ("mod", "proj0", "hgrn", "att0", "peer0", "proj1", "att1", "peer1", "fin")


def trunk(nc, dram, phases=PHASES):
    core = Core(nc, dram)
    with ExitStack() as ctx:
        def keep(name, shape):
            return ctx.enter_context(nc.sbuf_tensor(name, shape, F32))

        core.h = keep("h", [P, NT, D])
        core.vecs = keep("vecs", [P, V_ALL])
        core.ident = keep("ident", [P, P])
        core.ones = keep("ones", [P, P])
        core.eps = keep("eps", [P, 1])
        core.modc = keep("modc", [P, 2, 2, 48])
        core.ring = keep("ring", [P, RING * 2 * D])
        core.silu = keep("silu", [P, DC, 4])
        core.pairs = ctx.enter_context(nc.sbuf_tensor("pairs", [4, 2], F32))
        core.lb = keep("lb", [P, 8])
        if "mod" in phases:
            modulation(core)
        with ExitStack() as layer:
            featT = features(core, FEAT0)
            tokV = layer.enter_context(nc.sbuf_tensor("tokV0", [P, NT, TOK0], F32))
            with ExitStack() as scan:
                sums = scan.enter_context(nc.sbuf_tensor("logf_sums", [P, 2 * HG_HEADS, NT, P + 1], F32))
                if "proj0" in phases:
                    project(core, 0, FEAT0, featT, tokV, TOK0, 0, sums)
                if "hgrn" in phases:
                    hgrn(core, featT, tokV, sums)
            if "att0" in phases:
                attention(core, 0, featT, tokV)
        if "peer0" in phases:
            peer(core, 0)
        with ExitStack() as layer:
            featT = features(core, FEAT1)
            tokV = layer.enter_context(nc.sbuf_tensor("tokV1", [P, NT, TOK1], F32))
            if "proj1" in phases:
                project(core, 1, FEAT1, featT, tokV, TOK1, 8)
            if "att1" in phases:
                attention(core, 1, featT, tokV)
        if "peer1" in phases:
            peer(core, 1)
        if "fin" in phases:
            final_norm(core)


def shape_constants():
    c = np.zeros((P, C_ALL), np.float32)
    c[:, C_ID:C_ID + P] = np.eye(P)
    for base, head in ((C_ROT_SW, 64), (C_ROT_GA, 128)):
        half = head // 2
        for m in range(P):
            if m % head < half:
                c[m + half, base + m] = -1.0
            else:
                c[m - half, base + m] = 1.0
    t, s = np.arange(P)[:, None], np.arange(P)[None, :]
    c[:, C_WL:C_WL + P] = np.where(s >= t, 0.0, -1e30)
    c[:, C_WR:C_WR + P] = np.where(s <= t, 0.0, -1e30)
    c[:, C_IOTA:C_IOTA + 16] = 16.0 * np.arange(16)
    c[:, C_IOTA + 16:C_IOTA + 32] = np.arange(16)
    key = np.arange(P)
    for l, m in enumerate(SPAN):
        same, half = key // (2 * m), key // m
        c[:, C_HGM + P * l:C_HGM + P * l + P] = (same[:, None] == same) & (half[:, None] != half)
    c[:, C_HGM + P * LEVELS:C_HGM + P * LEVELS + P] = np.eye(P)
    tok = np.arange(NX)
    row, colm = (tok // 64).astype(np.float32), (tok % 64).astype(np.float32)
    for head, cc, cs in ((64, C_SW_COS, C_SW_SIN), (128, C_GA_COS, C_GA_SIN)):
        nf = head // 4
        inv = np.float32(10000.0) ** (-np.arange(nf, dtype=np.float32) / np.float32(nf))
        ang = np.concatenate([row[:, None] * inv, colm[:, None] * inv], axis=-1).T
        ang = np.tile(ang, (P // (head // 2), 1))
        c[:, cc:cc + NX] = np.cos(ang)
        c[:, cs:cs + NX] = np.sin(ang)
    return c


def laid_out(i):
    a = {}

    def col(v):
        return np.asarray(v).reshape(-1, P).T

    a["x"] = i["x"][0]
    a["ctx"] = i["ctx"][0]
    a["ada_w"] = i["ada_w"]
    cc = np.stack([col(i["c"][0]), col(i["c_ctx"])], axis=2).reshape(P, 16)
    pos_head = [(p // 2) + 4 * (p % 2) for p in range(8)]
    a["vecs"] = np.concatenate([
        cc, col(i["ada_b"][0]), col(i["ada_b"][1]), col(i["norm_mix_g"][0]), col(i["norm_mix_g"][1]),
        col(i["norm_ffn_g"][0]), col(i["norm_ffn_g"][1]), col(i["hg_lb_logits"][0]), col(i["hg_lb_logits"][1]),
        col(i["hg_norm_g"][0]), col(i["ga_q_norm_g"][0]), col(i["ga_k_norm_g"][0]),
        np.broadcast_to(i["sw_sink"][0][pos_head], (P, 8))], axis=1)
    w = i["ab_w_in"][0]
    q0 = 5 * HG_W
    sq = [w[:, q0 + 64 * h:q0 + 64 * h + 64] for h in pos_head]
    feat = np.concatenate([w[:, 0:3 * HG_W], w[:, 4 * HG_W:5 * HG_W]] + sq + [w[:, q0 + 512:q0 + 640]], axis=1)
    a["wf0"] = feat.reshape(DC, P, FEAT0, P).transpose(2, 1, 0, 3).reshape(FEAT0, P, D)
    tok = np.concatenate([w[:, 3 * HG_W:4 * HG_W], w[:, q0 + 640:q0 + 768]], axis=1)
    a["wt0"] = tok.reshape(DC, P, TOK0).transpose(1, 0, 2).reshape(P, DC * TOK0)
    w = i["ga_w_in"][0]
    a["wf1"] = w[:, 0:10 * P].reshape(DC, P, FEAT1, P).transpose(2, 1, 0, 3).reshape(FEAT1, P, D)
    a["wt1"] = w[:, 10 * P:].reshape(DC, P, TOK1).transpose(1, 0, 2).reshape(P, DC * TOK1)
    wo = i["ab_w_out"][0]
    a["wo0"] = np.concatenate([wo[0:HG_W]] + [wo[HG_W + 64 * h:HG_W + 64 * h + 64] for h in pos_head], axis=0)
    a["wo1"] = i["ga_w_out"][0]
    for l in range(2):
        a[f"wq{l}"] = i["peer_w_q"][l]
        a[f"skT{l}"] = i["peer_sub_keys"][l].reshape(2 * PH, KEYS, P).transpose(0, 2, 1)
        a[f"uv{l}"] = np.concatenate([i["peer_u"][l], i["peer_v"][l]], axis=1)
    a["final_g"] = i["final_norm_g"]
    a["consts"] = shape_constants()
    return {k: np.ascontiguousarray(v) for k, v in a.items()}


def build(nc, arrays, phases=PHASES):
    dram = {k: nc.dram_tensor(f"in_{k}", v.shape, mybir.dt.from_np(v.dtype), kind="ExternalInput").ap()
            for k, v in arrays.items()}
    dram["out"] = nc.dram_tensor("out_y", (NX, D), F32, kind="ExternalOutput").ap()
    dram["modr"] = nc.dram_tensor("modr", (2, 2, 6 * D), F32, kind="Internal").ap()
    trunk(nc, dram, phases)


def kernel(**inputs):
    import concourse.bacc as bacc
    from concourse.bass_utils import run_bass_kernel_spmd

    arrays = laid_out({k: np.asarray(v) for k, v in inputs.items()})
    nc = bacc.Bacc("TRN2", target_bir_lowering=False, num_devices=1)
    build(nc, arrays)
    r = run_bass_kernel_spmd(nc, [{f"in_{k}": v for k, v in arrays.items()}], core_ids=[0])
    return r.results[0]["out_y"].reshape(1, NX, D)
```
